# Optimizing a Trainium2 kernel written in Bass

```python
import math
import jax, jax.numpy as jnp
from jax import lax
import numpy as np

D_MODEL = 1024
BATCH = 1
SEQ = 512
DEPTH = 1

RWKV_HEAD = 64
D_RWKV = D_MODEL // 2
N_RWKV_HEADS = D_RWKV // RWKV_HEAD
DECAY_LORA = 64
AAA_LORA = 64
GATE_LORA = 160
LN_X_EPS = 64e-5
D_CONV = D_MODEL // 2
CONV_WIDTH = 3
N_MEM = 256
N_XHEADS = 4
XHEAD_DIM = D_MODEL // N_XHEADS
D_FF = 4 * D_MODEL
RMS_EPS = 1e-6

SPLITS = (D_RWKV, D_RWKV, D_RWKV, DECAY_LORA, AAA_LORA, GATE_LORA,
          D_CONV, D_CONV, D_CONV,
          D_MODEL, D_MODEL)
D_IN = sum(SPLITS)
RWKV_COLS = 3 * D_RWKV + DECAY_LORA + AAA_LORA + GATE_LORA


def rms_norm(x, g):
    xf = x.astype(jnp.float32)
    y = xf * lax.rsqrt(jnp.mean(xf * xf, axis=-1, keepdims=True) + RMS_EPS)
    return (y * g.astype(jnp.float32)).astype(x.dtype)

def token_shift(p):
    return jnp.pad(p[:, :-1], ((0, 0), (1, 0), (0, 0)))

def wkv7_scan(r, w, k, v, a, b):
    bsz, _, h, n = r.shape

    def step(state, inp):
        r_t, w_t, k_t, v_t, a_t, b_t = inp
        sa = jnp.einsum("bhvk,bhk->bhv", state, a_t)
        state = (state * w_t[:, :, None, :]
                 + sa[..., None] * b_t[:, :, None, :]
                 + v_t[..., None] * k_t[:, :, None, :])
        return state, jnp.einsum("bhvk,bhk->bhv", state, r_t)

    xs = tuple(jnp.moveaxis(t, 1, 0) for t in (r, w, k, v, a, b))
    s0 = jnp.zeros((bsz, h, n, n), jnp.float32)
    _, ys = lax.scan(step, s0, xs)
    return jnp.moveaxis(ys, 0, 1)

def rwkv7_branch(r, k, v, wd, ad, gd, w0, w_lora_w, a0, w_lora_a, w_lora_g,
                 k_k, k_a, r_k, ln_x_w, ln_x_b):
    bsz, s, _ = r.shape
    f32 = jnp.float32
    log_w = -jax.nn.softplus(-(w0 + jnp.tanh(wd) @ w_lora_w)) - 0.5
    decay = jnp.exp(-jnp.exp(log_w.astype(f32)))
    a = jax.nn.sigmoid(a0 + ad @ w_lora_a)
    g = jax.nn.sigmoid(gd) @ w_lora_g

    def heads(t):
        return t.reshape(bsz, s, N_RWKV_HEADS, RWKV_HEAD).astype(f32)

    kk = heads(k * k_k)
    kk = kk / jnp.maximum(jnp.sqrt(jnp.sum(kk * kk, axis=-1, keepdims=True)), 1e-12)
    k = k * (1.0 + (a - 1.0) * k_a)
    rh, kh, vh, ah, wh = heads(r), heads(k), heads(v), heads(a), heads(decay)
    y = wkv7_scan(rh, wh, kh, vh, -kk, kk * ah)
    mu = jnp.mean(y, axis=-1, keepdims=True)
    var = jnp.mean(jnp.square(y - mu), axis=-1, keepdims=True)
    y = (y - mu) * lax.rsqrt(var + LN_X_EPS)
    y = y.reshape(bsz, s, D_RWKV) * ln_x_w.astype(f32) + ln_x_b.astype(f32)
    bonus = jnp.sum(rh * kh * r_k.astype(f32), axis=-1, keepdims=True) * vh
    y = y + bonus.reshape(bsz, s, D_RWKV)
    return y.astype(r.dtype) * g

def short_conv_branch(bg, cg, xc, conv_w):
    u = cg * xc
    y = lax.conv_general_dilated(
        u, conv_w.astype(u.dtype), window_strides=(1,),
        padding=[(CONV_WIDTH - 1, 0)],
        dimension_numbers=("NWC", "WIO", "NWC"),
        feature_group_count=D_CONV)
    return bg * y

def memory_cross_attention(h, mem_n, w_q, w_kv, w_xo):
    bsz, s, _ = h.shape
    n_mem = mem_n.shape[1]
    q = (h @ w_q).reshape(bsz, s, N_XHEADS, XHEAD_DIM)
    k, v = jnp.split(mem_n @ w_kv, 2, axis=-1)
    k = k.reshape(bsz, n_mem, N_XHEADS, XHEAD_DIM)
    v = v.reshape(bsz, n_mem, N_XHEADS, XHEAD_DIM)
    scores = jnp.einsum("bshd,bmhd->bhsm", q, k).astype(jnp.float32) / math.sqrt(XHEAD_DIM)
    probs = jax.nn.softmax(scores, axis=-1).astype(v.dtype)
    o = jnp.einsum("bhsm,bmhd->bshd", probs, v).reshape(bsz, s, D_MODEL)
    return o @ w_xo

def first_inputs(seed: int = 0) -> dict:
    key = jax.random.key(seed)
    ks = jax.random.split(key, 32)
    it = iter(range(32))
    f32 = jnp.float32
    L = DEPTH

    def nrm(shape, scale):
        return scale * jax.random.normal(ks[next(it)], shape, f32)

    def gain(shape):
        return 1.0 + 0.05 * jax.random.normal(ks[next(it)], shape, f32)

    return {
        "x": nrm((BATCH, SEQ, D_MODEL), 1.0),
        "mem": nrm((BATCH, N_MEM, D_MODEL), 1.0),
        "norm_mix": gain((L, D_MODEL)),
        "w_in": nrm((L, D_MODEL, D_IN), D_MODEL ** -0.5),
        "b_gate": nrm((L, 2 * D_MODEL), 0.01),
        "mu_shift": jax.random.uniform(ks[next(it)], (L, RWKV_COLS), f32),
        "w0": jax.random.uniform(ks[next(it)], (L, D_RWKV), f32, -6.0, -1.0),
        "w_lora_w": nrm((L, DECAY_LORA, D_RWKV), 0.1 * DECAY_LORA ** -0.5),
        "a0": nrm((L, D_RWKV), 0.1),
        "w_lora_a": nrm((L, AAA_LORA, D_RWKV), AAA_LORA ** -0.5),
        "w_lora_g": nrm((L, GATE_LORA, D_RWKV), GATE_LORA ** -0.5),
        "k_k": 0.85 + nrm((L, D_RWKV), 0.05),
        "k_a": gain((L, D_RWKV)),
        "r_k": nrm((L, N_RWKV_HEADS, RWKV_HEAD), 0.1),
        "ln_x_w": gain((L, D_RWKV)),
        "ln_x_b": nrm((L, D_RWKV), 0.01),
        "conv_w": nrm((L, CONV_WIDTH, 1, D_CONV), CONV_WIDTH ** -0.5),
        "w_proj_a": nrm((L, D_RWKV, D_MODEL), D_RWKV ** -0.5),
        "w_proj_b": nrm((L, D_CONV, D_MODEL), D_CONV ** -0.5),
        "w_out_mix": nrm((L, D_MODEL, D_MODEL), D_MODEL ** -0.5),
        "norm_xattn": gain((L, D_MODEL)),
        "norm_mem": gain((L, D_MODEL)),
        "w_q": nrm((L, D_MODEL, D_MODEL), D_MODEL ** -0.5),
        "w_kv": nrm((L, D_MODEL, 2 * D_MODEL), D_MODEL ** -0.5),
        "w_xo": nrm((L, D_MODEL, D_MODEL), D_MODEL ** -0.5),
        "norm_mlp": gain((L, D_MODEL)),
        "w_up": nrm((L, D_MODEL, D_FF), D_MODEL ** -0.5),
        "w_down": nrm((L, D_FF, D_MODEL), D_FF ** -0.5),
        "norm_final": gain((D_MODEL,)),
    }

def first_block(x, mem, norm_mix, w_in, b_gate, mu_shift, w0, w_lora_w, a0, w_lora_a,
              w_lora_g, k_k, k_a, r_k, ln_x_w, ln_x_b, conv_w, w_proj_a, w_proj_b,
              w_out_mix, norm_xattn, norm_mem, w_q, w_kv, w_xo, norm_mlp, w_up,
              w_down, norm_final):
    offsets = np.cumsum(SPLITS)[:-1].tolist()
    for i in range(DEPTH):
        h = rms_norm(x, norm_mix[i])
        p = h @ w_in[i]
        p_rw = p[..., :RWKV_COLS]
        p_rw = p_rw + (token_shift(p_rw) - p_rw) * mu_shift[i]
        p = jnp.concatenate([p_rw, p[..., RWKV_COLS:]], axis=-1)
        r, k, v, wd, ad, gd, cb, cc, cx, ga, gb = jnp.split(p, offsets, axis=-1)
        out_a = rwkv7_branch(r, k, v, wd, ad, gd, w0[i], w_lora_w[i], a0[i], w_lora_a[i],
                             w_lora_g[i], k_k[i], k_a[i], r_k[i], ln_x_w[i], ln_x_b[i])
        out_b = short_conv_branch(cb, cc, cx, conv_w[i])
        bg_a, bg_b = jnp.split(b_gate[i], 2)
        merged = (jax.nn.sigmoid(ga + bg_a) * (out_a @ w_proj_a[i])
                  + jax.nn.sigmoid(gb + bg_b) * (out_b @ w_proj_b[i]))
        x = x + merged @ w_out_mix[i]
        mem_n = rms_norm(mem, norm_mem[i])
        x = x + memory_cross_attention(rms_norm(x, norm_xattn[i]), mem_n,
                                       w_q[i], w_kv[i], w_xo[i])
        hm = rms_norm(x, norm_mlp[i])
        x = x + jnp.square(jax.nn.relu(hm @ w_up[i])) @ w_down[i]
    return rms_norm(x, norm_final)


HEAD_DIM = 64
N_Q_HEADS = 8
N_KV_HEADS = 2
GQ = N_Q_HEADS // N_KV_HEADS
WINDOW = 128
BLOCK = 128
ROPE_THETA = 10000.0
D_A = N_Q_HEADS * HEAD_DIM
D_KV = N_KV_HEADS * HEAD_DIM

CHUNK = 128
N_GROUPS = 4
D_B = D_MODEL // 2
GROUP_W = D_B // N_GROUPS

EPS = 1e-6
NEG = -1e30

SPLIT_SIZES = [D_A, D_KV, D_KV, D_A,
               D_B, D_B, D_B,
               2 * D_MODEL]
SPLIT_IDX = [int(s) for s in np.cumsum(SPLIT_SIZES)[:-1]]
D_IN_2 = int(sum(SPLIT_SIZES))


def _rms(x, g):
    xf = x.astype(jnp.float32)
    y = xf * lax.rsqrt(jnp.mean(xf * xf, axis=-1, keepdims=True) + EPS)
    return (y * g.astype(jnp.float32)).astype(x.dtype)

def _layernorm(x, g, b):
    xf = x.astype(jnp.float32)
    mu = jnp.mean(xf, axis=-1, keepdims=True)
    var = jnp.mean(jnp.square(xf - mu), axis=-1, keepdims=True)
    y = (xf - mu) * lax.rsqrt(var + EPS)
    return (y * g.astype(jnp.float32) + b.astype(jnp.float32)).astype(x.dtype)

def _rope(t, positions):
    half = HEAD_DIM // 2
    inv_freq = ROPE_THETA ** (-jnp.arange(half, dtype=jnp.float32) / half)
    ang = positions.astype(jnp.float32)[..., None] * inv_freq
    cos = jnp.cos(ang)[:, :, None, :]
    sin = jnp.sin(ang)[:, :, None, :]
    tf = t.astype(jnp.float32)
    t1, t2 = tf[..., :half], tf[..., half:]
    out = jnp.concatenate([t1 * cos - t2 * sin, t2 * cos + t1 * sin], axis=-1)
    return out.astype(t.dtype)

def _band(t):
    b, s, h, d = t.shape
    tb = t.reshape(b, s // BLOCK, BLOCK, h, d)
    prev = jnp.pad(tb[:, :-1], ((0, 0), (1, 0), (0, 0), (0, 0), (0, 0)))
    return jnp.concatenate([prev, tb], axis=2)

def _swa_with_sinks(q, k, v, sinks):
    b, s = q.shape[:2]
    nb = s // BLOCK
    qb = q.reshape(b, nb, BLOCK, N_KV_HEADS, GQ, HEAD_DIM)
    kb, vb = _band(k), _band(v)
    scores = jnp.einsum('bnqkgd,bnjkd->bnkgqj', qb, kb).astype(jnp.float32)
    scores = scores * (1.0 / math.sqrt(HEAD_DIM))
    qi = jnp.arange(BLOCK)[:, None]
    kj = jnp.arange(2 * BLOCK)[None, :]
    rel = qi + BLOCK - kj
    in_win = (rel >= 0) & (rel < WINDOW)
    blk = jnp.arange(nb)[:, None, None]
    valid = in_win[None] & ((blk > 0) | (kj[None] >= BLOCK))
    scores = jnp.where(valid[None, :, None, None], scores, NEG)
    sink = sinks.astype(jnp.float32).reshape(N_KV_HEADS, GQ)[None, None, :, :, None, None]
    sink = jnp.broadcast_to(sink, scores.shape[:-1] + (1,))
    probs = jax.nn.softmax(jnp.concatenate([scores, sink], axis=-1), axis=-1)[..., :-1]
    out = jnp.einsum('bnkgqj,bnjkd->bnqkgd', probs.astype(v.dtype), vb)
    return out.reshape(b, s, N_Q_HEADS * HEAD_DIM)

def _chunked_spatial_gating(u, v, ln_g, ln_b, w_s, b_s):
    b, s, _ = v.shape
    nc = s // CHUNK
    vn = _layernorm(v, ln_g, ln_b).reshape(b, nc, CHUNK, N_GROUPS, GROUP_W)
    causal = jnp.tril(jnp.ones((CHUNK, CHUNK), dtype=bool))
    w = jnp.where(causal[None], w_s, jnp.zeros((), w_s.dtype))
    sv = jnp.einsum('gts,bnsgc->bntgc', w, vn) + b_s.T[None, None, :, :, None]
    return u * sv.reshape(b, s, D_B)

def second_inputs(seed: int = 0) -> dict:
    key = jax.random.key(seed)
    ks = jax.random.split(key, 18)
    f32 = jnp.float32
    nrm = lambda k, shape, s: jax.random.normal(k, shape, f32) * s
    x = jax.random.normal(ks[0], (BATCH, SEQ, D_MODEL), f32)
    c = jax.random.normal(ks[1], (BATCH, D_MODEL), f32)
    positions = jnp.broadcast_to(jnp.arange(SEQ, dtype=jnp.int32), (BATCH, SEQ))
    return {
        "x": x,
        "c": c,
        "positions": positions,
        "w_ada": nrm(ks[2], (DEPTH, D_MODEL, 3 * D_MODEL), 0.5 * D_MODEL ** -0.5),
        "b_ada": nrm(ks[3], (DEPTH, 3 * D_MODEL), 0.02),
        "g_pre": 1.0 + nrm(ks[4], (DEPTH, D_MODEL), 0.05),
        "g_post": 1.0 + nrm(ks[5], (DEPTH, D_MODEL), 0.05),
        "w_in": nrm(ks[6], (DEPTH, D_MODEL, D_IN_2), D_MODEL ** -0.5),
        "sinks": nrm(ks[7], (DEPTH, N_Q_HEADS), 1.0),
        "ln_v_g": 1.0 + nrm(ks[8], (DEPTH, D_B), 0.05),
        "ln_v_b": nrm(ks[9], (DEPTH, D_B), 0.02),
        "w_s": nrm(ks[10], (DEPTH, N_GROUPS, CHUNK, CHUNK), CHUNK ** -0.5),
        "b_s": 1.0 + nrm(ks[11], (DEPTH, N_GROUPS, CHUNK), 0.1),
        "w_proj_a": nrm(ks[12], (DEPTH, D_A, D_MODEL), D_A ** -0.5),
        "w_proj_b": nrm(ks[13], (DEPTH, D_B, D_MODEL), D_B ** -0.5),
        "w_out": nrm(ks[14], (DEPTH, D_MODEL, D_MODEL), D_MODEL ** -0.5),
    }

def second_block(x, c, positions, w_ada, b_ada, g_pre, g_post, w_in, sinks,
              ln_v_g, ln_v_b, w_s, b_s, w_proj_a, w_proj_b, w_out):
    b, s, _ = x.shape
    c_act = jax.nn.silu(c)
    for l in range(DEPTH):
        ada = (c_act @ w_ada[l] + b_ada[l])[:, None, :]
        shift, scale, gate = jnp.split(ada, 3, axis=-1)
        h = _rms(x, g_pre[l]) * (1.0 + scale) + shift

        proj = h @ w_in[l]
        q, k, v, z_a, u_b, v_b, z_b, g_logits = jnp.split(proj, SPLIT_IDX, axis=-1)

        q = _rope(q.reshape(b, s, N_Q_HEADS, HEAD_DIM), positions)
        k = _rope(k.reshape(b, s, N_KV_HEADS, HEAD_DIM), positions)
        v = v.reshape(b, s, N_KV_HEADS, HEAD_DIM)
        y_a = _swa_with_sinks(q, k, v, sinks[l]) * jax.nn.silu(z_a)

        y_b = _chunked_spatial_gating(jax.nn.gelu(u_b, approximate=False),
                                      jax.nn.gelu(v_b, approximate=False),
                                      ln_v_g[l], ln_v_b[l], w_s[l], b_s[l])
        y_b = y_b * jax.nn.silu(z_b)

        gates = jax.nn.sigmoid(g_logits)
        gate_a, gate_b = jnp.split(gates, 2, axis=-1)
        merged = gate_a * (y_a @ w_proj_a[l]) + gate_b * (y_b @ w_proj_b[l])
        y = merged @ w_out[l]

        x = x + gate * _rms(y, g_post[l])
    return x


def setup_inputs(seed=0):
    out = dict(first_inputs(seed))
    for name, value in second_inputs(seed + 1).items():
        if name != "x":
            out[name + "_2"] = value
    return out


def reference(
    x, mem, norm_mix, w_in, b_gate, mu_shift, w0, w_lora_w, a0, w_lora_a, w_lora_g, k_k, k_a,
    r_k, ln_x_w, ln_x_b, conv_w, w_proj_a, w_proj_b, w_out_mix, norm_xattn, norm_mem, w_q, w_kv,
    w_xo, norm_mlp, w_up, w_down, norm_final, c_2, positions_2, w_ada_2, b_ada_2, g_pre_2,
    g_post_2, w_in_2, sinks_2, ln_v_g_2, ln_v_b_2, w_s_2, b_s_2, w_proj_a_2, w_proj_b_2,
    w_out_2,
):
    x = first_block(
        x, mem, norm_mix, w_in, b_gate, mu_shift, w0, w_lora_w, a0, w_lora_a, w_lora_g, k_k,
        k_a, r_k, ln_x_w, ln_x_b, conv_w, w_proj_a, w_proj_b, w_out_mix, norm_xattn, norm_mem,
        w_q, w_kv, w_xo, norm_mlp, w_up, w_down, norm_final,
    )
    return second_block(
        x, c_2, positions_2, w_ada_2, b_ada_2, g_pre_2, g_post_2, w_in_2, sinks_2, ln_v_g_2,
        ln_v_b_2, w_s_2, b_s_2, w_proj_a_2, w_proj_b_2, w_out_2,
    )


_drawn_inputs = setup_inputs


def setup_inputs(seed=0):
    import zlib

    import numpy as np

    out = dict(_drawn_inputs(seed))
    spreads = {}
    factors = {'b_gate': 8.0,
     'w_lora_w': 8.0,
     'a0': 5.54,
     'k_k': 4.368,
     'k_a': 3.78,
     'ln_x_w': 3.972,
     'ln_x_b': 8.0,
     'norm_xattn': 8.0,
     'norm_mem': 7.122,
     'g_post_2': 4.049,
     'sinks_2': 8.0,
     'ln_v_g_2': 7.999,
     'ln_v_b_2': 34.478,
     'b_s_2': 2.737,
     'norm_mlp': 3.776}
    for name, (base, spread) in spreads.items():
        noise = np.random.default_rng([zlib.crc32(name.encode()), seed]).standard_normal(out[name].shape)
        drawn = base * np.exp(spread * noise) if base else spread * noise
        out[name] = __import__('jax').numpy.asarray(drawn.astype(out[name].dtype))
    for name, factor in factors.items():
        out[name] = (out[name] * factor).astype(out[name].dtype)
    return out
```

```python
import concourse.bass as bass
from concourse import mybir
from concourse.alu_op_type import AluOpType as ALU
import numpy as np

F32, F32R, I32 = mybir.dt.float32, mybir.dt.float32r, mybir.dt.int32
ACT = mybir.ActivationFunctionType
AX = mybir.AxisListType

S = 512
D = 1024
NP = 128
KT = D // NP
N_MEM = 256
HEADS, HD = 8, 64
HALF = D // 2
FT = HALF // NP
L = 64
NC = S // L
XH, XD = 4, 256
EPS = 1e-6
LNX_EPS = 64e-5
DECAY = float(np.exp(np.float32(-0.5)))
NEG = -1e30

N_RW = 15
CONV0 = N_RW
GATE0 = CONV0 + 3 * FT
Q2, KD2, V2, UB, VB, ZA, ZB, G2 = 0, 4, 6, 7, 11, 15, 19, 23
N_IN2 = 39
WKV_PANELS = 6

VECS = [("norm_mix", 8), ("b_gate", 16), ("mu", 15), ("a0", 4), ("k_k", 4), ("k_a", 4), ("r_k", 4),
        ("ln_x_w", 4), ("ln_x_b", 4), ("conv_w", 12), ("norm_xattn", 8), ("norm_mem", 8),
        ("norm_mlp", 8), ("norm_final", 8), ("g_pre", 8), ("g_post", 8), ("b_ada", 24), ("c", 8),
        ("inv_freq", 1)]
COL = {}
_n = 0
for _name, _w in VECS:
    COL[_name] = _n
    _n += _w
N_VEC = _n
LEVELS = [1, 2, 4, 8, 16, 32]
MATS = [("ident", 128), ("mean", 128), ("head_sum", 128), ("cumsum", 128), ("chunk_mask", 128),
        ("rotate", 128), ("causal", 128), ("eye", 64)] + [(f"level{s}", 64) for s in LEVELS]
MAT = {}
_n = 0
for _name, _w in MATS:
    MAT[_name] = (_n, _w)
    _n += _w
N_MAT = _n


def constants():
    i, j = np.arange(128)[:, None], np.arange(128)[None, :]
    j64 = np.arange(64)[None, :]
    same = (i // 64) == (j // 64)
    out = {
        "ident": i == j,
        "mean": np.full((128, 128), 1.0 / D),
        "head_sum": same,
        "cumsum": same & (i <= j),
        "chunk_mask": np.where(j < 64, (i % 64) < (j % 64), (i % 64) <= (j % 64)),
        "rotate": np.where((j % 64) < 32, -1.0 * (i == j + 32), 1.0 * (i == j - 32)),
        "causal": i <= j,
        "eye": (i % 64) == j64,
    }
    for s in LEVELS:
        ii = i % 64
        out[f"level{s}"] = (ii // (2 * s) == j64 // (2 * s)) & ((ii // s) % 2 == 1) & ((j64 // s) % 2 == 0)
    return np.concatenate([out[n].astype(np.float32) for n, _ in MATS], axis=1)


def window_masks():
    q, j = np.arange(128)[:, None], np.arange(256)[None, :]
    rel = q + 128 - j
    ok = (rel >= 0) & (rel < 128)
    first = ok & (j >= 128)
    return np.concatenate([np.where(first, 0.0, NEG), np.where(ok, 0.0, NEG)], axis=1).astype(np.float32)


class Loops:
    running = []


class Mark:

    def __init__(self, counter):
        self.sem, self.n = counter.sem, counter.n
        self.per = [(lo, lo["per"].get(counter.name, 0)) for lo in Loops.running]

    def of_round(self, i):
        m = object.__new__(Mark)
        m.sem, m.n, m.per = self.sem, self.n + i * self.per[-1][1], self.per[:-1]
        return m

    def value(self):
        v = self.n
        for lo, per in self.per:
            assert any(x is lo for x in Loops.running), "a mark of a loop that has ended"
            if per:
                v = lo["i"] * per + v
        return v


class Lane:

    def __init__(self, nc, queue, name):
        self.q, self.name, self.sem, self.n = queue, name, nc.alloc_semaphore("done_" + name), 0
        self.met = {}
        self.passed = Passed(nc, name) if name in ("pe", "pool") else None

    def did(self, ins):
        ins.then_inc(self.sem, 1)
        self.n += 1
        return Mark(self)

    def now(self):
        return Mark(self)

    def ago(self, d):
        m = Mark(self)
        m.n -= d
        return m

    def need(self, *marks):
        for m in marks:
            if m is None or (m.n == 0 and not m.per):
                continue
            key, n = (id(m.sem), *(id(lo) for lo, _ in m.per)), self.met.get(id(m.sem), (None, -1))
            if n[0] == (key, len(Loops.running)) and n[1] >= m.n:
                continue
            self.met[id(m.sem)] = ((key, len(Loops.running)), m.n)
            self.wait(m.sem, m.value())

    def wait(self, sem, value):
        self.q.wait_ge(sem, value)
        if self.passed is not None and not isinstance(value, int):
            self.q.sem_inc(self.passed.sem, 1)
            self.passed.n += 1


class Passed:

    def __init__(self, nc, name):
        self.name, self.sem, self.n = name + "_passed", nc.alloc_semaphore(name + "_waits_passed"), 0


class loop:

    def __init__(self, nc, lanes, count, **per):
        self.nc, self.lanes, self.count, self.per = nc, lanes, count, per

    def __enter__(self):
        lanes = self.lanes
        self.ctx = self.nc.Fori(0, self.count, engines=(
            mybir.EngineType.PE, mybir.EngineType.Activation, mybir.EngineType.DVE, mybir.EngineType.Pool))
        i = self.ctx.__enter__()
        self.entry = {"i": i, "per": self.per}
        self.start = {x.name: x.n for x in lanes}
        self.forget()
        Loops.running.append(self.entry)
        return i

    def forget(self):
        for x in self.lanes:
            if isinstance(x, Lane):
                x.met.clear()

    def __exit__(self, *e):
        self.ctx.__exit__(*e)
        self.forget()
        if e[0] is not None:
            return False
        Loops.running.pop()
        got = {x.name: x.n - self.start[x.name] for x in self.lanes if x.n != self.start[x.name]}
        self.per.update({k: v for k, v in got.items() if k.endswith("_passed")})
        want = {k: v for k, v in self.per.items() if v}
        assert got == want, f"a round raises {got}, not {want}"
        for x in self.lanes:
            x.n = self.start[x.name] + self.count * self.per.get(x.name, 0)
        return False


def tile(t, m):
    if isinstance(m, int):
        return t[:, m, :]
    return t[:, bass.ds(m, 1), :].rearrange("p a n -> p (a n)")


def build(nc, x_in, mem_in, panels, ada_w, vec_in, mat_in, win_in, lora_in, pos_in, sink_in, ws_in,
          lnv_in, bs_in, out, stop=None, dbg=None):
    T = Lane(nc, nc.tensor, "pe")
    A = Lane(nc, nc.scalar, "act")
    V = Lane(nc, nc.vector, "dve")
    G = Lane(nc, nc.gpsimd, "pool")

    def tt(E, o, a, b, op, *after):
        E.need(*after)
        return E.did(E.q.tensor_tensor(o, a, b, op))

    def ts(E, o, a, s1, op0, s2, op1, *after):
        E.need(*after)
        if op1 is None:
            return E.did(E.q.tensor_scalar(o, a, s1, None, op0))
        return E.did(E.q.tensor_scalar(o, a, s1, s2, op0, op1))

    def stt(o, a, s, b, op0, op1, *after):
        V.need(*after)
        return V.did(V.q.scalar_tensor_tensor(o, a, s, b, op0, op1))

    def act(o, a, f, *after, **kw):
        A.need(*after)
        return A.did(A.q.activation(o, a, f, **kw))

    def copy(E, o, a, *after):
        E.need(*after)
        if E is A:
            return A.did(A.q.activation(o, a, ACT.Copy))
        return E.did(E.q.tensor_copy(o, a))

    def inv_sqrt(dst, src, scale, op, eps, *after):
        m = ts(V, dst, src, scale, ALU.mult, eps, op, *after)
        V.need(act(dst, dst, ACT.Sqrt, m))
        return V.did(V.q.reciprocal(dst, dst))

    def fill(E, o, v, *after):
        E.need(*after)
        return E.did(E.q.memset(o, v))

    def mm(o, lhsT, rhs, start=True, stop=True):
        return nc.tensor.matmul(o, lhsT, rhs, start=start, stop=stop, skip_group_check=True)

    at = [(nc.sbuf_base + 31) // 32 * 32]

    def region(nbytes):
        a = at[0]
        at[0] += (nbytes + 31) // 32 * 32
        assert at[0] <= nc.sbuf_usable_end, f"sbuf {at[0]}"
        return a

    def place(name, shape, offset, dt=F32):
        return nc.alloc_sbuf_tensor_at(name, shape, dt, offset=offset)

    TB = S * 4
    r_x, r_opA, r_opB = region(KT * TB), region(2 * KT * TB), region(2 * KT * TB)
    r_w = region(6 * KT * NP * 4)
    r_p = region(N_IN2 * TB)
    r_rstd, r_pad, r_tmp, r_sq, r_acc = region(TB), region(2 * (S + 8) * 4), region(2 * TB), region(2 * TB), region(TB)
    r_mat, r_vec = region(N_MAT * 4), region(N_VEC * 4)
    r_col = region(56 * 4)
    r_pb, r_st = region(NC * (L + 1) * 4), region(3 * L * 4)

    xT = place("xT", [NP, KT, S], r_x)
    opA = [place(f"opA_{p}", [NP, KT, S], r_opA + n * KT * TB, F32R) for n, p in enumerate(("hi", "lo"))]
    opB = [place(f"opB_{p}", [NP, KT, S], r_opB + n * KT * TB, F32R) for n, p in enumerate(("hi", "lo"))]
    WB = KT * NP * 4
    w_raw = place("w_raw", [NP, 2, KT * NP], r_w)
    w_hi = [place(f"w_hi{j}", [NP, KT, NP], r_w + (2 + j) * WB, F32R) for j in range(2)]
    w_lo = [place(f"w_lo{j}", [NP, KT, NP], r_w + (4 + j) * WB, F32R) for j in range(2)]
    P = place("P", [NP, N_IN2, S], r_p)
    rstd = place("rstd", [NP, S], r_rstd)
    pad = [place(f"pad{j}", [NP, S + 2], r_pad + j * (S + 8) * 4) for j in range(2)]
    tmp = [place(f"tmp{j}", [NP, S], r_tmp + j * TB) for j in range(2)]
    sq = [place(f"sq{j}", [NP, S], r_sq + j * TB) for j in range(2)]
    acc = place("acc", [NP, S], r_acc)
    acc2, r1 = place("acc2", [NP, S], r_pad), place("rstd_first", [NP, S], r_pad + TB)
    mats = place("mats", [NP, N_MAT], r_mat)
    vecs = place("vecs", [NP, N_VEC], r_vec)
    cols = place("cols", [NP, 56], r_col)
    adac, gain2, gate2, silc, gain3 = (cols[:, a:b] for a, b in ((0, 24), (24, 32), (32, 40), (40, 48), (48, 56)))

    def mat(name):
        a, w = MAT[name]
        return mats[:, a:a + w]

    def vec(name, m=0):
        c = m + COL[name]
        return vecs[:, c:c + 1] if isinstance(c, int) else vecs[:, bass.ds(c, 1)]

    bank = [nc.alloc_psum_tensor(f"bank{b}", [NP, S], F32) for b in range(8)]

    def load(name, *pairs, queue=nc.scalar):
        class arrived:
            sem, n = nc.alloc_semaphore("loaded_" + name), 16 * len(pairs)
        arrived.name = name
        for o, i in pairs:
            queue.dma_start(o, i).then_inc(arrived.sem, 16)
        return Mark(arrived)

    def tiled(ap):
        return ap.rearrange("(k p) n -> p k n", p=NP)

    m_const = load("constants", (vecs[:, :], vec_in), (mats[:, :], mat_in))
    m_x = [load(f"x{q}", (xT[:, 2 * q:2 * q + 2, :], tiled(x_in)[:, 2 * q:2 * q + 2, :]),
                queue=(nc.scalar, nc.gpsimd)[q % 2]) for q in range(4)]
    lw = place("lora_w", [65, HALF], r_p + 15 * TB)
    la = place("lora_a", [NP, HALF], r_p + 16 * TB)
    lg = [place("lora_g0", [NP, HALF], r_p + 17 * TB), place("lora_g1", [32, HALF], r_p + 18 * TB)]
    m_lora = load("lora", (lw[:, :], lora_in[0:65, :]), (la[64:128, :], lora_in[65:129, :]),
                  (lg[0][:, :], lora_in[129:257, :]), (lg[1][:, :], lora_in[257:289, :]))

    s_raw = [nc.alloc_semaphore(f"raw_panel_in_slot{j}") for j in range(2)]
    s_hi, s_lo = nc.alloc_semaphore("high_parts_made"), nc.alloc_semaphore("low_parts_made")
    s_mm, s_free = nc.alloc_semaphore("panels_multiplied"), nc.alloc_semaphore("banks_freed")
    nc.vector.sem_inc(s_lo, 2)
    nc.vector.sem_inc(s_free, 2)
    nc.tensor.sem_inc(s_mm, 2)
    n_panels = panels.shape[0]

    class panel_no:
        name, n = "panels", 0
    lanes = [T, A, V, G, panel_no, T.passed, G.passed]


    def panel_value(ahead=0, half=False):
        v = panel_no.n + ahead
        v = v // 2 if half else v
        for lo in Loops.running:
            per = lo["per"].get("panels", 0)
            assert per % 2 == 0
            if per:
                v = lo["i"] * (per // 2 if half else per) + v
        return v

    stops = dict(shift=16, lora=16, wkv=40, merged=52, x1=60, x2=92, x3=156, h2=156, p2=196, swa=196, y=196)
    with nc.sync.Fori(0, stops.get(stop, n_panels) // 2) as h:
        for j in range(2):
            nc.sync.wait_ge(s_lo, h * 2 + (j + 1))
            nc.sync.dma_start(w_raw[:, j, :],
                              panels[bass.ds(h * 2 + j, 1), :, :].rearrange("a p n -> p (a n)")).then_inc(s_raw[j], 16)

    def split(ahead):
        j = (panel_no.n + ahead) % 2
        flat = "p k n -> p (k n)"
        A.q.wait_ge(s_raw[j], panel_value(ahead, half=True) * 16 + 16)
        A.q.wait_ge(s_mm, panel_value(ahead) + 1)
        A.q.activation(w_hi[j][:, :, :].rearrange(flat), w_raw[:, j, :], ACT.Copy).then_inc(s_hi, 1)
        V.q.wait_ge(s_hi, panel_value(ahead) + 1)
        V.q.tensor_tensor(w_lo[j][:, :, :].rearrange(flat), w_raw[:, j, :],
                          w_hi[j][:, :, :].rearrange(flat).bitcast(F32), ALU.subtract).then_inc(s_lo, 1)

    def panel(op, leave, n=S, two=False, last=False, ready=None, between=None):
        steps = panel_steps(op, leave, n, two, last, ready, between)
        for made in steps:
            pass
        return made

    def panel_steps(op, leave, n=S, two=False, last=False, ready=None, between=None):
        j = panel_no.n % 2
        T.q.wait_ge(s_lo, panel_value() + 3)
        T.q.wait_ge(s_free, panel_value() + 1)
        hi, lo = op
        ps = [bank[j], bank[2 + j]] if two else [bank[j]]
        if not last:
            split(1)
        for k in range(KT):
            if ready:
                T.need(ready[k])
            o = ps[k // (KT // 2) if two else 0][:, 0:n]
            first, end = k % (KT // 2 if two else KT) == 0, (k + 1) % (KT // 2 if two else KT) == 0
            nc.tensor.matmul(o, w_hi[j][:, k, :], hi[:, k, 0:n], start=first, stop=False)
            nc.tensor.matmul(o, w_hi[j][:, k, :], lo[:, k, 0:n], start=False, stop=False)
            ins = nc.tensor.matmul(o, w_lo[j][:, k, :], hi[:, k, 0:n], start=False, stop=end)
            if k < KT - 1:
                yield None
        ins.then_inc(s_mm, 1)
        if between:
            between()
        V.q.wait_ge(s_mm, panel_value() + 3)
        A.q.wait_ge(s_mm, panel_value() + 3)

        def freed(ins):
            ins.then_inc(s_free, 1)

        def out_of_psum(E):
            E.wait(s_free, panel_value() + 3)

        made = leave([p[:, 0:n] for p in ps], freed, out_of_psum, j)
        panel_no.n += 1
        yield made

    def segment(count, op, make, n=S, two=False, last=0, ready=None, between=None, **per):
        made = []

        def some(ms, **kw):
            before = [A.now(), V.now(), G.now()]
            for m in ms:
                made.append(panel(op, make(m, before), n=n, two=two, **kw))
                kw.pop("between", None)

        first = 2 if ready or between else 0
        if first:
            some(range(2), ready=ready, between=between)
        pairs = (count - first) // 2 - (1 if last else 0)
        if pairs > 0:
            with loop(nc, lanes, pairs, panels=2, **{k: 2 * v for k, v in per.items()}) as i:
                some([i * 2 + (j + first) for j in range(2)])
            round_marks = [made.pop() for _ in range(2)][::-1]
            made += [m and m.of_round(i) for i in range(pairs) for m in round_marks]
        if last:
            some([count - 2])
            some([count - 1], last=True)
        elif count % 2:
            some([count - 1])
        return made

    def leave_plain(dst, scale_by, base=0):
        def make(m, before):
            def leave(ps, freed, out, j):
                freed(V.q.tensor_tensor(tile(dst, m + base), ps[0], scale_by, ALU.mult))
            return leave
        return make

    def leave_copy(base):
        def make(m, before):
            def leave(ps, freed, out, j):
                freed(V.q.tensor_copy(tile(P, m + base), ps[0]))
            return leave
        return make

    def scaled(ps, freed, out, j, before):
        V.need(*before)
        freed(V.q.tensor_tensor(tmp[j][:, :], ps[0], rstd[:, :], ALU.mult))

    def leave_function(base, f):
        def make(m, before):
            def leave(ps, freed, out, j):
                freed(A.q.activation(tile(P, m + base), ps[0], f))
            return leave
        return make

    def leave_silu(base):
        def make(m, before):
            def leave(ps, freed, out, j):
                V.need(act(sq[j][:, :], ps[0], ACT.Sigmoid, *before))
                freed(V.q.tensor_tensor(tile(P, m + base), ps[0], sq[j][:, :], ALU.mult))
            return leave
        return make

    def leave_shift(base):
        def make(m, before):
            def leave(ps, freed, out, j):
                V.need(*before)
                freed(V.q.tensor_tensor(pad[j][:, 1:S + 1], ps[0], rstd[:, :], ALU.mult))
                out(G)
                d = tt(G, tmp[j][:, :], pad[j][:, 0:S], pad[j][:, 1:S + 1], ALU.subtract)
                stt(tile(P, m + base), tmp[j][:, :], vec("mu", m), pad[j][:, 1:S + 1], ALU.mult, ALU.add, d)
            return leave
        return make

    def square_sum(src, j, gain, op, m, *after, n=S):
        h = act(tile(op[0], m)[:, 0:n], src, ACT.Copy, *after, scale=gain)
        lo = stt(tile(op[1], m)[:, 0:n], src, gain, tile(op[0], m)[:, 0:n].bitcast(F32), ALU.mult, ALU.subtract, h)
        s = act(sq[j][:, 0:n], src, ACT.Square)
        tt(G, acc[:, 0:n], acc[:, 0:n], sq[j][:, 0:n], ALU.add, s, G.now())
        return lo

    def leave_residual(gain=None, op=None):
        def make(m, before):
            def leave(ps, freed, out, j):
                freed(V.q.tensor_tensor(tile(xT, m), ps[0], tile(xT, m), ALU.add))
                if gain:
                    out(A)
                    out(V)
                    return square_sum(tile(xT, m), j, vec(gain, m), op, m, *before)
            return leave
        return make

    def rms(eps=EPS, n=S, dst=rstd, mean=None):
        T.need(G.now())
        m = T.did(mm(bank[7][:, 0:n], mat("mean"), acc[:, 0:n]))
        r = inv_sqrt(dst[:, 0:n], bank[7][:, 0:n], 1.0, ALU.add, eps, m)
        fill(G, acc[:, :], 0.0, m)
        V.need(r)

    def two_parts(op, m, src, *after):
        h = act(tile(op[0], m), src, ACT.Copy, *after)
        return tt(V, tile(op[1], m), src, tile(op[0], m).bitcast(F32), ALU.subtract, h, *after)

    def done(src_ap):
        s = nc.alloc_semaphore("dbg")
        for E in (T, A, V, G):
            nc.gpsimd.wait_ge(E.sem, E.n)
        nc.gpsimd.wait_ge(s_free, panel_no.n + 2)
        for E in (T, G):
            nc.gpsimd.wait_ge(E.passed.sem, E.passed.n)
        for j in range(2):
            nc.gpsimd.wait_ge(s_raw[j], 8 * stops[stop])
        nc.gpsimd.dma_start(dbg, src_ap).then_inc(s, 16)
        nc.gpsimd.wait_ge(s, 16)

    fill(G, acc[:, :], 0.0)
    fill(G, pad[0][:, 0:1], 0.0)
    fill(G, pad[1][:, 0:1], 0.0)
    for E in (T, A, V, G):
        E.need(m_const)
    split(0)
    ready = []
    for k in range(KT):
        x = xT[:, k, :]
        h = act(opA[0][:, k, :], x, ACT.Copy, m_x[k // 2], scale=vec("norm_mix", k))
        ready.append(stt(opA[1][:, k, :], x, vec("norm_mix", k), opA[0][:, k, :].bitcast(F32), ALU.mult,
                         ALU.subtract, m_x[k // 2], h))
        q = tt(G, sq[k % 2][:, :], x, x, ALU.mult, m_x[k // 2], G.now())
        tt(G, acc[:, :], acc[:, :], sq[k % 2][:, :], ALU.add, q)

    segment(N_RW, opA, leave_shift(0), pool=1, dve=1, ready=ready, between=rms)
    if stop == "shift":
        return done(P[:, 0:N_RW, :])

    r_sg, r_cum, r_a, r_g = (r_opB + n * FT * TB for n in range(4))
    sg = place("decay_sigmoid", [NP, FT, HALF], r_sg)
    cum = place("decay_sums", [NP, FT, S], r_cum)
    aa = place("a", [NP, FT, S], r_a)
    gg = place("g", [NP, FT, S], r_g)
    th = place("tanh_wd", [65, S], r_p + 19 * TB)
    fill(V, th[64:65, :], 1.0)
    t1 = act(th[0:64, :], P[0:64, 12, :], ACT.Tanh, V.now())
    t2 = act(P[:, 13, :], P[:, 13, :], ACT.Sigmoid, V.now())
    act(P[0:32, 14, :], P[0:32, 14, :], ACT.Sigmoid)
    T.need(m_lora, A.now(), G.now(), V.now())
    free = {}
    for t in range(FT):
        b = 2 + t % 2
        T.need(free.get(b))
        m = T.did(mm(bank[b][:, :], th[:, t * NP:(t + 1) * NP], lw[:, :]))
        free[b] = act(sg[:, t, :], bank[b][:, :], ACT.Sigmoid, m)
    for f in range(FT):
        b = 4 + f % 2
        T.need(free.get(b))
        m = T.did(mm(bank[b][:, :], la[64:128, f * NP:(f + 1) * NP], P[64:128, 12, :]))
        free[b] = act(aa[:, f, :], bank[b][:, :], ACT.Sigmoid, m, bias=vec("a0", f))
    for f in range(FT):
        b = 6 + f % 2
        T.need(free.get(b))
        mm(bank[b][:, :], lg[0][:, f * NP:(f + 1) * NP], P[:, 13, :], True, False)
        m = T.did(mm(bank[b][:, :], lg[1][:, f * NP:(f + 1) * NP], P[0:32, 14, :], False, True))
        free[b] = copy(V, gg[:, f, :], bank[b][:, :], m)
    for f in range(FT):
        b = 2 + f % 2
        T.need(free.get(b), A.now())
        for t in range(FT):
            m = mm(bank[b][:, t * NP:(t + 1) * NP], sg[:, t, f * NP:(f + 1) * NP], mat("cumsum"))
        m = T.did(m)
        free[b] = copy(V, cum[:, f, :], bank[b][:, :], m)
    if stop == "lora":
        return done(cum[:, :, :])

    AR = place("AR", [NP, NC, 2 * L], r_x)
    BKt = place("BK_t", [NP, NC, NP], r_x + 4096)
    GT = place("GT", [NP, NC, 2, 2 * L], r_x + 8192)
    w4 = [place(f"work{n}", [NP, S], r_x + 8192 + n * TB) for n in range(4)]
    BK = place("BK", [NP, NC, 2 * L], r_sg)
    At = place("A_t", [NP, NC, L], r_sg)
    UV = place("UV", [NP, NC, NP], r_sg + 4096)
    X = place("X", [NP, NC, L], r_p + 12 * TB)
    XT = place("XT", [NP, NC, L], r_p + 13 * TB)
    Y = place("Y", [NP, NC, L], r_p + 14 * TB)
    Z = place("Z", [NP, NC, L], r_pad)
    WT = place("WT", [NP, NC, L], r_pad + TB)
    ABT = place("ABT", [NP, NC, L], r_sq)
    vs = place("v_copy", [NP, S], r_sq + TB)
    Pb = place("P_chunk", [NP, NC, L + 1], r_pb)
    st = [place(f"state{n}", [NP, L], r_st + n * L * 4) for n in range(2)]
    st_p = place("state_decayed", [NP, L], r_st + 2 * L * 4)
    HH = [(0, 64), (64, 128)]
    C8 = "p (c l) -> p c l"

    def c8(ap):
        return ap.rearrange(C8, c=NC)

    def wide(name, n):
        a, w = MAT[name]
        return mats[:, a:a + w].unsqueeze(1).broadcast_to([NP, n, w])

    fill(G, Pb[:, :, 0:1], 1.0)

    counts = dict(pe=WKV_PE, act=WKV_ACT, dve=WKV_DVE, pool=WKV_POOL)
    with loop(nc, lanes, FT, panels=WKV_PANELS, **counts) as f:
        start = [T.now(), A.now(), V.now(), G.now()]
        rt, kt, vt = tile(P, f), tile(P, f + 4), tile(P, f + 8)
        at_, ct = tile(aa, f), tile(cum, f)
        made = [0]

        def filler(count=1):
            for _ in range(count):
                e = made[0]
                if e >= WKV_PANELS:
                    return
                before = [A.now(), V.now(), G.now()]
                if e < 3:
                    step = leave_plain(P, rstd[:, :])(f * 3 + (CONV0 + e), before)
                else:
                    m = f * 3 + (e - 3)

                    def step(ps, freed, out_, j, m=m, before=before):
                        scaled(ps, freed, out_, j, before)
                        out_(A)
                        A.did(A.q.activation(tile(P, m + GATE0), tmp[j][:, :], ACT.Sigmoid, bias=vec("b_gate", m)))
                panel(opA, step)
                made[0] += 1

        kk, t_b, kp, pinv = w4
        for E in (A, V, G, T):
            E.need(*start)
        p1 = act(Pb[:, :, 1:L + 1], c8(ct), ACT.Exp, scale=-DECAY)
        p2 = act(pinv[:, :], ct, ACT.Exp, scale=DECAY)
        k1 = ts(V, kk[:, :], kt, vec("k_k", f), ALU.mult, None, None)
        k2 = act(t_b[:, :], kk[:, :], ACT.Square, k1)
        T.need(k2)
        k3 = T.did(mm(bank[2][:, :], mat("head_sum"), t_b[:, :]))
        vcopy = copy(G, vs[:, :], vt)
        kp1 = ts(V, kp[:, :], at_, -1.0, ALU.add, vec("k_a", f), ALU.mult)
        filler()
        k4 = inv_sqrt(t_b[:, :], bank[2][:, :], 1.0, ALU.max, 1e-24, k3)
        k5 = tt(V, kk[:, :], kk[:, :], t_b[:, :], ALU.mult, k4)
        kp2 = stt(kp[:, :], kp[:, :], 1.0, kt, ALU.add, ALU.mult, kp1)
        ar1 = stt(AR[:, :, 0:L], c8(kk[:, :]), -1.0, Pb[:, :, 0:L], ALU.mult, ALU.mult, k5, p1)
        ar2 = tt(G, AR[:, :, L:2 * L], c8(rt), Pb[:, :, 1:L + 1], ALU.mult, p1)
        b1 = tt(G, t_b[:, :], kk[:, :], at_, ALU.mult, k5)
        b2 = tt(G, BK[:, :, 0:L], c8(t_b[:, :]), c8(pinv[:, :]), ALU.mult, b1, p2)
        b3 = tt(V, BK[:, :, L:2 * L], c8(kp[:, :]), c8(pinv[:, :]), ALU.mult, kp2, p2)
        bo1 = stt(t_b[:, :], rt, vec("r_k", f), kp[:, :], ALU.mult, ALU.mult, kp2, b2)
        T.need(bo1, k4)
        bo2 = T.did(mm(bank[2][:, :], mat("head_sum"), t_b[:, :]))
        bo3 = tt(V, rt, bank[2][:, :], vt, ALU.mult, bo2, ar2)

        T.need(ar1, ar2, b2, b3)
        for dst, left, right in ((3, AR, BK), (4, BK, AR)):
            for c in range(NC):
                for h, (lo, hi) in enumerate(HH):
                    ins = mm(bank[dst][lo:hi, c * L:(c + 1) * L], left[lo:hi, c, 0:L], right[lo:hi, c, 0:L])
            m = T.did(ins)
            if dst == 3:
                x1 = tt(V, X[:, :, :], c8(bank[3][:, :]), wide("level1", NC), ALU.mult, m)
                x2 = tt(V, X[:, :, :], X[:, :, :], wide("eye", NC), ALU.add, x1)
            else:
                abt = copy(A, ABT[:, :, :], c8(bank[4][:, :]), m)
        T.need(x2)
        for c in range(NC):
            for lo, hi in HH:
                ins = mm(bank[5][lo:hi, c * L:(c + 1) * L], X[lo:hi, c, :], mat("ident")[lo:hi, lo:hi])
        m = T.did(ins)
        xt = copy(A, XT[:, :, :], c8(bank[5][:, :]), m)
        g_free = {6: V.now(), 7: V.now(), 2: bo3, 3: x1}
        for r in range(2):
            bb = ((6, 7), (2, 3))[r]
            T.need(g_free[bb[0]], g_free[bb[1]])
            for q in range(4):
                for h, (lo, hi) in enumerate(HH):
                    ins = mm(bank[bb[h]][:, q * NP:(q + 1) * NP], BK[lo:hi, 4 * r + q, :], AR[lo:hi, 4 * r + q, :])
            m = T.did(ins)
            V.need(bo3, b3)
            for h in range(2):
                gt = tt(V, GT[:, 4 * r:4 * r + 4, h, :], bank[bb[h]][:, :].rearrange("p (a l) -> p a l", a=4),
                        wide("chunk_mask", 4), ALU.mult, m)
                g_free[bb[h]] = gt
        g_free[5] = xt
        g_free[4] = abt
        bt = []
        for r in range(2):
            b = (5, 4)[r]
            T.need(g_free[b])
            for q in range(4):
                ins = nc.tensor.transpose(bank[b][:, q * NP:(q + 1) * NP], BK[:, 4 * r + q, :], mat("ident"))
            m = T.did(ins)
            g_free[b] = copy(A, BKt[:, 4 * r:4 * r + 4, :], bank[b][:, :].rearrange("p (a l) -> p a l", a=4), m)
        bkt = g_free[4]
        for r in range(2):
            b = (6, 7)[r]
            T.need(g_free[b], vcopy)
            for q in range(4):
                c = 4 * r + q
                ins = mm(bank[b][64:128, q * NP:(q + 1) * NP], vs[:, c * L:(c + 1) * L], mat("ident"))
            m = T.did(ins)
            g_free[b] = copy(A, UV[64:128, 4 * r:4 * r + 4, :],
                             bank[b][64:128, :].rearrange("p (a l) -> p a l", a=4), m)
        uv = g_free[7]
        T.need(g_free[2])
        for c in range(NC):
            for lo, hi in HH:
                ins = mm(bank[2][lo:hi, c * L:(c + 1) * L], AR[lo:hi, c, 0:L], mat("ident")[lo:hi, lo:hi])
        m = T.did(ins)
        at_m = g_free[2] = copy(V, At[:, :, :], c8(bank[2][:, :]), m)

        xd = {0: [x2, xt, abt], 1: [x2, xt, abt]}
        yb_free = {0: [g_free[2], g_free[3]], 1: [g_free[4], g_free[5]]}
        for s in LEVELS[1:]:
            lastl = s == LEVELS[-1]
            ym = {}
            for g in range(2):
                cs, b = range(4 * g, 4 * g + 4), 2 + 2 * g
                T.need(*xd[g], *yb_free[g])
                for n, c in enumerate(cs):
                    for lo, hi in HH:
                        ins = mm(bank[b][lo:hi, n * L:(n + 1) * L], ABT[lo:hi, c, :], X[lo:hi, c, :])
                m = T.did(ins)
                ym[g] = tt(V, Y[:, 4 * g:4 * g + 4, :], bank[b][:, 0:4 * L].rearrange("p (c l) -> p c l", c=4),
                           wide(f"level{s}", 4), ALU.mult, m)
            for g in range(2):
                cs, b = range(4 * g, 4 * g + 4), 3 + 2 * g
                T.need(ym[g])
                if not lastl:
                    for n, c in enumerate(cs):
                        for lo, hi in HH:
                            mm(bank[b][lo:hi, n * L:(n + 1) * L], XT[lo:hi, c, :], Y[lo:hi, c, :])
                for n, c in enumerate(cs):
                    for lo, hi in HH:
                        ins = mm(bank[b][lo:hi, (4 + n) * L:(5 + n) * L], Y[lo:hi, c, :], XT[lo:hi, c, :])
                m = T.did(ins)
                dst = slice(4 * g, 4 * g + 4)
                d = [tt(V, XT[:, dst, :], XT[:, dst, :],
                        bank[b][:, 4 * L:8 * L].rearrange("p (c l) -> p c l", c=4), ALU.add, m)]
                if not lastl:
                    d.append(tt(V, X[:, dst, :], X[:, dst, :],
                                bank[b][:, 0:4 * L].rearrange("p (c l) -> p c l", c=4), ALU.add, m))
                xd[g] = d
                yb_free[g] = d
            if s == 4:
                filler()

        T.need(uv, gt, *xd[0], *xd[1], at_m, bkt)
        for c in range(NC):
            for h, (lo, hi) in enumerate(HH):
                ins = mm(bank[6][lo:hi, c * L:(c + 1) * L], GT[64:128, c, h, 0:L], UV[64:128, c, lo:hi])
        m = T.did(ins)
        z = copy(V, Z[:, :, :], c8(bank[6][:, :]), m)
        for c in range(NC):
            for h, (lo, hi) in enumerate(HH):
                ins = mm(bank[7][lo:hi, c * L:(c + 1) * L], At[lo:hi, c, :], XT[lo:hi, c, :])
        m = T.did(ins)
        wt = copy(A, WT[:, :, :], c8(bank[7][:, :]), m)

        s0 = fill(G, st[0][:, :], 0.0)
        sready, s_free_b = s0, {4: None, 5: None}
        u = []
        T.need(z, wt, g_free[6])
        for c in range(NC):
            bs = 4 + c % 2
            T.need(*u)
            for h, (lo, hi) in enumerate(HH):
                mm(bank[2 + h][0:L, 0:L], XT[lo:hi, c, :], Z[lo:hi, c, :], True, False)
            T.need(sready)
            for h, (lo, hi) in enumerate(HH):
                ins = mm(bank[2 + h][0:L, 0:L], WT[lo:hi, c, :], st[c % 2][lo:hi, :], False, True)
            m = T.did(ins)
            u = [copy((A, V)[h], UV[0:L, c, lo:hi], bank[2 + h][0:L, 0:L], m) for h, (lo, hi) in enumerate(HH)]
            if c < NC - 1:
                sp = act(st_p[:, :], st[c % 2][:, :], ACT.Copy, sready, V.now(), scale=Pb[:, c, L:L + 1])
                T.need(*u, s_free_b[bs])
                for h, (lo, hi) in enumerate(HH):
                    ins = mm(bank[bs][lo:hi, 0:L], BKt[:, c, lo:hi], UV[:, c, lo:hi])
                m = T.did(ins)
                V.need(T.now())
            else:
                T.need(*u)
            for h, (lo, hi) in enumerate(HH):
                mm(bank[6][lo:hi, c * L:(c + 1) * L], st[c % 2][lo:hi, :], AR[lo:hi, c, L:2 * L], start=(c == 0), stop=False)
            for h, (lo, hi) in enumerate(HH):
                ins = mm(bank[6][lo:hi, c * L:(c + 1) * L], UV[:, c, lo:hi], GT[:, c, h, L:2 * L], start=False,
                         stop=(c == NC - 1))
            ym_ = T.did(ins)
            if c < NC - 1:
                sready = stt(st[1 - c % 2][:, :], bank[bs][:, 0:L], Pb[:, c, L:L + 1], st_p[:, :],
                             ALU.mult, ALU.add, m, sp)
                s_free_b[bs] = sready
            if c in (0, 2, 4, 6):
                filler()

        y, ysq, v1_, v2_ = w4
        y1 = copy(A, y[:, :], bank[6][:, :], ym_)
        T.need(y1)
        m = T.did(mm(bank[2][:, :], mat("head_sum"), y[:, :]))
        y2 = stt(y[:, :], bank[2][:, :], -1.0 / HD, y[:, :], ALU.mult, ALU.add, m)
        y3 = act(ysq[:, :], y[:, :], ACT.Square, y2)
        T.need(y3)
        m = T.did(mm(bank[3][:, :], mat("head_sum"), ysq[:, :]))
        y5 = inv_sqrt(v1_[:, :], bank[3][:, :], 1.0 / HD, ALU.add, LNX_EPS, m)
        y6 = tt(V, y[:, :], y[:, :], v1_[:, :], ALU.mult, y5)
        y7 = ts(V, y[:, :], y[:, :], vec("ln_x_w", f), ALU.mult, vec("ln_x_b", f), ALU.add, y6)
        y8 = tt(V, y[:, :], y[:, :], rt, ALU.add, y7, bo3)
        y9 = tt(V, tile(gg, f), tile(gg, f), y[:, :], ALU.mult, y8)
        filler(WKV_PANELS)
    if stop == "wkv":
        return done(gg[:, :, :])

    A.need(V.now(), T.now())
    m_x = load("x_again", (xT[:, :, :], tiled(x_in)))
    fill(V, pad[0][:, 0:2], 0.0, A.now(), V.now(), T.now(), G.now())
    fill(V, pad[1][:, 0:2], 0.0)
    for f in range(FT):
        m = 3 * FT + f

        def step(ps, freed, out_, j, m=m, f=f):
            scaled(ps, freed, out_, j, [A.now(), V.now()])
            out_(A)
            A.did(A.q.activation(P[:, m - 3 * FT, :], tmp[j][:, :], ACT.Sigmoid, bias=vec("b_gate", m)))
            u = pad[j]
            cb, cc, cx = (P[:, CONV0 + 3 * f + n, :] for n in range(3))
            c0 = tt(V, u[:, 2:S + 2], cc, cx, ALU.mult, V.now())
            c1 = ts(V, cc, u[:, 0:S], vec("conv_w", f), ALU.mult, None, None, c0)
            c2 = stt(cc, u[:, 1:S + 1], vec("conv_w", 4 + f), cc, ALU.mult, ALU.add, c1)
            c3 = stt(cc, u[:, 2:S + 2], vec("conv_w", 8 + f), cc, ALU.mult, ALU.add, c2)
            tt(V, cb, cb, cc, ALU.mult, c3)
        panel(opA, step)

    A.q.wait_ge(s_mm, panel_no.n + 2)
    V.q.wait_ge(s_mm, panel_no.n + 2)
    ready = [two_parts(opA, f, gg[:, f, :], V.now()) for f in range(FT)]
    ready += [two_parts(opA, 4 + f, P[:, CONV0 + 3 * f, :], V.now()) for f in range(FT)]

    def gate_tile(g):
        return GATE0 + g if g < 3 * FT else g - 3 * FT

    def leave_merge(ga, gb, op):
        def make(m, before):
            def leave(ps, freed, out_, j):
                V.need(*before)
                g1 = V.did(V.q.tensor_tensor(tmp[j][:, :], ps[0], tile(P, m + ga), ALU.mult))
                freed(V.q.tensor_tensor(sq[j][:, :], ps[1], tile(P, m + gb), ALU.mult))
                out_(G)
                g3 = tt(G, tmp[j][:, :], tmp[j][:, :], sq[j][:, :], ALU.add, g1)
                return two_parts(op, m, tmp[j][:, :], g3)
            return leave
        return make

    merged = []
    for b0, n in ((0, 4), (4, 4)):
        def make(m, before, b0=b0):
            return leave_merge(GATE0, gate_tile(8 + b0) - b0, opB)(m + b0, before)
        merged += segment(n, opA, make, two=True, ready=None if b0 else ready, act=1, dve=2, pool=1)
    if stop == "merged":
        T.need(A.now(), V.now())
        return done(opB[0][:, :, :].bitcast(F32))

    memT = place("memT", [NP, KT, N_MEM], r_p)
    memo = [place(f"mem_{p}", [NP, KT, N_MEM], r_p + (4 + 4 * n) * TB, F32R) for n, p in enumerate(("hi", "lo"))]
    kvT = place("kvT", [NP, 2 * KT, N_MEM], r_p + 12 * TB)
    vtm = place("v_mem", [NP, 2, D], r_p + 20 * TB)
    qT = place("qT", [NP, KT, S], r_p + 24 * TB)
    rstd_m = place("rstd_mem", [NP, N_MEM], r_pad)
    A.need(V.now())
    m_mem = load("mem", (memT[:, :, :], tiled(mem_in)))
    V.need(m_x)
    A.need(m_x)
    attn_in = segment(KT, opB, leave_residual("norm_xattn", opA), ready=merged, act=2, dve=1, pool=1)
    rms()
    A.need(m_mem)
    with loop(nc, lanes, KT // 2, act=4, dve=2, pool=2) as i:
        before = [G.now(), V.now()]
        for j in range(2):
            square_sum(tile(memT, i * 2 + j), j, vec("norm_mem", i * 2 + j), memo, i * 2 + j, *before, n=N_MEM)
    rms(n=N_MEM, dst=rstd_m)
    T.need(A.now(), V.now())
    if stop == "x1":
        return done(xT[:, :, :])

    segment(2 * KT, memo, leave_plain(kvT, rstd_m[:, :]), n=N_MEM)
    segment(KT, opA, leave_plain(qT, rstd[:, :]))
    for E in (T, A, V):
        E.q.wait_ge(s_free, panel_no.n + 2)
    for mt in range(2):
        b = 2 + mt
        for g in range(2):
            for q in range(4):
                ins = nc.tensor.transpose(bank[b + 2 * g][:, q * NP:(q + 1) * NP],
                                          kvT[:, KT + 4 * g + q, mt * NP:(mt + 1) * NP], mat("ident"))
            m = T.did(ins)
            copy(A, vtm[:, mt, g * 512:(g + 1) * 512], bank[b + 2 * g][:, :], m)

    ex = [place(f"exp{n}", [NP, 4, N_MEM], r_p + (32 + 2 * n) * TB) for n in range(2)]
    pT = [place(f"probs_t{n}", [NP, 2, S], r_p + (0 if n else 36) * TB) for n in range(2)]
    stat = [place(f"stat{n}", [NP, 16], r_pb + n * 64) for n in range(2)]
    XS = XD ** -0.5
    score_free, tr_free, pv_free = {}, {}, {}
    sm, prob = {}, {}

    def scores(h):
        n, e = h % 2, ex[h % 2]
        mx, nm, su, rs = (stat[n][:, 4 * q:4 * q + 4] for q in range(4))
        ms = []
        for half in range(2):
            b = 2 * n + half
            T.need(score_free.get(b))
            for q in range(2):
                t = 2 * half + q
                for d in range(2):
                    ins = mm(bank[b][:, q * N_MEM:(q + 1) * N_MEM], qT[:, 2 * h + d, t * NP:(t + 1) * NP],
                             kvT[:, 2 * h + d, :], start=(d == 0), stop=(d == 1))
            m = T.did(ins)
            V.need(m, *([sm[h - 2]] if h >= 2 else []))
            ms.append(V.did(V.q.reduce_max(mx[:, 2 * half:2 * half + 2],
                                           bank[b][:, :].rearrange("p (t m) -> p t m", t=2), AX.X)))
        nmm = ts(V, nm, mx, -XS, ALU.mult, None, None, *ms)
        for t in range(4):
            b = 2 * n + t // 2
            A.need(nmm, prob.get(h - 2))
            score_free[b] = A.did(A.q.activation(e[:, t, :], bank[b][:, (t % 2) * N_MEM:(t % 2 + 1) * N_MEM], ACT.Exp,
                                                 bias=nm[:, t:t + 1], scale=XS, accum_out=su[:, t:t + 1]))
        V.need(score_free[2 * n + 1])
        r = V.did(V.q.reciprocal(rs, su))
        sm[h] = tt(V, e[:, :, :], e[:, :, :], rs.unsqueeze(2).broadcast_to([NP, 4, N_MEM]), ALU.mult, r)

    def weigh(h):
        n = h % 2
        T.need(sm[h])
        pts = []
        for mt in range(2):
            b = 4 + mt
            T.need(tr_free.get(b))
            for t in range(4):
                ins = nc.tensor.transpose(bank[b][:, t * NP:(t + 1) * NP], ex[n][:, t, mt * NP:(mt + 1) * NP], mat("ident"))
            m = T.did(ins)
            prob[h] = m
            tr_free[b] = copy(A if mt else V, pT[n][:, mt, :], bank[b][:, :], m, pv_free.get((h - 2, 1)))
            pts.append(tr_free[b])
        for d in range(2):
            b = 6 + d
            T.need(*pts, pv_free.get((h - 1, d, "out")))
            for mt in range(2):
                c = h * XD + d * NP
                ins = mm(bank[b][:, :], vtm[:, mt, c:c + NP], pT[n][:, mt, :], start=(mt == 0), stop=(mt == 1))
            m = T.did(ins)
            pv_free[(h, 1)] = m
            hi = act(opB[0][:, 2 * h + d, :], bank[b][:, :], ACT.Copy, m)
            pv_free[(h, d, "out")] = tt(V, opB[1][:, 2 * h + d, :], bank[b][:, :],
                                        opB[0][:, 2 * h + d, :].bitcast(F32), ALU.subtract, hi)

    T.need(A.now())
    scores(0)
    for h in range(XH):
        if h + 1 < XH:
            scores(h + 1)
        weigh(h)
    for E in (T, A, V):
        E.need(A.now(), V.now())

    mlp_in = segment(KT, opB, leave_residual("norm_mlp", opA), act=2, dve=1, pool=1)
    if stop == "x2":
        return done(xT[:, :, :])

    AW = 3 * D
    ada_sum = place("ada_sum", [NP, AW], r_p)
    ada_in = [place(f"ada_w{n}", [NP, AW], r_p + (6 + 6 * n) * TB) for n in range(2)]
    s_ada = [nc.alloc_semaphore(f"ada_rows{n}") for n in range(2)]
    c0 = act(silc, vecs[:, COL["c"]:COL["c"] + 8], ACT.Sigmoid)
    c1 = tt(V, silc, silc, vecs[:, COL["c"]:COL["c"] + 8], ALU.mult, c0)
    at_start = [c1, A.now(), V.now(), T.now()]

    def modulation():
        G.need(*at_start)
        for k in range(KT):
            n = k % 2
            if k >= 2:
                G.need(G.now())
            if k == 0:
                for q in range(2):
                    nc.gpsimd.dma_start(ada_in[q][:, :], ada_w[q * NP:(q + 1) * NP, :]).then_inc(s_ada[q], 16)
            nc.gpsimd.wait_ge(s_ada[n], 16 * (k // 2 + 1))
            if k == 0:
                ts(G, ada_sum[:, :], ada_in[0][:, :], silc[:, 0:1], ALU.mult, None, None)
            else:
                a1 = ts(G, ada_in[n][:, :], ada_in[n][:, :], silc[:, k:k + 1], ALU.mult, None, None, G.now())
                tt(G, ada_sum[:, :], ada_sum[:, :], ada_in[n][:, :], ALU.add, a1, G.now())
            if k + 2 < KT:
                G.need(G.now())
                nc.gpsimd.dma_start(ada_in[n][:, :], ada_w[(k + 2) * NP:(k + 3) * NP, :]).then_inc(s_ada[n], 16)

    hid = [place(f"hidden{j}", [NP, S], r_p + (24 + j) * TB) for j in range(2)]

    def leave_relu2(m, before):
        def leave(ps, freed, out_, j):
            V.need(*before)
            freed(V.q.scalar_tensor_tensor(tmp[j][:, :], ps[0], 0.0, rstd[:, :], ALU.max, ALU.mult))
            out_(A)
            out_(V)
            h = A.did(A.q.activation(opB[0][:, bass.ds(m, 1), :].rearrange("p a n -> p (a n)"), tmp[j][:, :], ACT.Square))
            h2 = tt(V, hid[j][:, :], tmp[j][:, :], tmp[j][:, :], ALU.mult)
            return tt(V, tile(opB[1], m), hid[j][:, :], tile(opB[0], m).bitcast(F32), ALU.subtract, h, h2)
        return leave

    def leave_relu2_make(m, before):
        return leave_relu2(m, [before[0], before[1]])

    segment(KT, opA, leave_relu2_make, act=1, dve=2, ready=mlp_in,
            between=lambda: (rms(), modulation()))
    hid_done = [2 * (KT - 1 - k) for k in range(KT)]
    with loop(nc, lanes, 3, panels=16, act=8, dve=16):
        segment(KT, opB, leave_residual(), ready=[V.ago(d) for d in hid_done])
        segment(KT, opA, leave_relu2_make, act=1, dve=2)

    hid_done = [V.ago(d) for d in hid_done]
    T.need(G.now())
    for c in range(24):
        ins = mm(bank[6][:, c:c + 1], ada_sum[:, c * NP:(c + 1) * NP], mat("mean")[:, 0:1])
    m = T.did(ins)
    d0 = stt(adac, bank[6][:, 0:24], float(D), vecs[:, COL["b_ada"]:COL["b_ada"] + 24], ALU.mult, ALU.add, m)
    d1 = stt(gain2, adac[:, 8:16], 1.0, vecs[:, COL["g_pre"]:COL["g_pre"] + 8], ALU.add, ALU.mult, d0)
    d3 = tt(V, gain3, gain2, vecs[:, COL["norm_final"]:COL["norm_final"] + 8], ALU.mult, d1)
    d2 = tt(V, gate2, adac[:, 16:24], vecs[:, COL["g_post"]:COL["g_post"] + 8], ALU.mult, d0)

    fill(G, acc2[:, :], 0.0, A.now(), V.now())

    def leave_x3(m, before):
        def leave(ps, freed, out_, j):
            freed(V.q.tensor_tensor(tile(xT, m), ps[0], tile(xT, m), ALU.add))
            out_(A)
            s1 = act(sq[j][:, :], tile(xT, m), ACT.Square, *before)
            s2 = act(tmp[j][:, :], tile(xT, m), ACT.Square, scale=vec("norm_final", m))
            tt(G, acc[:, :], acc[:, :], sq[j][:, :], ALU.add, s1, G.now())
            tt(G, acc2[:, :], acc2[:, :], tmp[j][:, :], ALU.add, s2, G.now())
        return leave
    segment(KT, opB, leave_x3, ready=hid_done, act=2, pool=2)
    if stop == "x3":
        return done(xT[:, :, :])

    T.need(G.now(), V.now())
    mm(bank[7][:, :], mat("mean"), acc[:, :])
    m1 = T.did(mm(bank[6][:, :], mat("mean"), acc2[:, :]))
    V.need(m1)
    e1 = ts(V, r1[:, :], bank[7][:, :], EPS, ALU.add, None, None)
    e2 = stt(rstd[:, :], r1[:, :], EPS, bank[6][:, :], ALU.mult, ALU.add, e1)
    e3 = act(rstd[:, :], rstd[:, :], ACT.Sqrt, e2)
    e4 = act(r1[:, :], r1[:, :], ACT.Sqrt)
    V.need(e3)
    r = V.did(V.q.reciprocal(rstd[:, :], rstd[:, :]))
    ready = []
    for k in range(KT):
        j = k % 2
        h0 = stt(tmp[j][:, :], xT[:, k, :], gain3[:, k:k + 1], rstd[:, :], ALU.mult, ALU.mult, r, A.now())
        h1 = act(opA[0][:, k, :], tmp[j][:, :], ACT.Identity, h0, bias=adac[:, k:k + 1])
        ready.append(stt(opA[1][:, k, :], tmp[j][:, :], adac[:, k:k + 1], opA[0][:, k, :].bitcast(F32), ALU.add,
                         ALU.subtract, h1))
    if stop == "h2":
        return done(opA[0][:, :, :].bitcast(F32))

    def x4():
        V.need(e4)
        m = V.did(V.q.reciprocal(r1[:, :], r1[:, :]))
        for k in range(KT):
            stt(xT[:, k, :], xT[:, k, :], vec("norm_final", k), r1[:, :], ALU.mult, ALU.mult, m)
    segment(7, opA, leave_copy(0), ready=ready, between=x4)
    segment(8, opA, leave_function(UB, ACT.Gelu))
    segment(8, opA, leave_silu(ZA), act=1)
    segment(16, opA, leave_function(G2, ACT.Sigmoid))
    for E in (T, A, V, G):
        E.q.wait_ge(s_free, panel_no.n + 2)
        E.need(A.now(), G.now())

    if stop == "p2":
        return done(P[:, :, :])

    o = r_opA
    def area(name, shape, dt=F32):
        nonlocal o
        t = place(name, shape, o, dt)
        n = 4
        for w in shape[1:]:
            n *= w
        o += (n + 31) // 32 * 32
        assert o <= r_opA + 2 * KT * TB
        return t
    ang, nr, cosT, sinT = (area(f"rope{n}", [NP, S]) for n in range(4))
    posi = place("positions_i", [NP, S], r_tmp, I32)
    kd = [area(f"k_dup{g}", [NP, NP + S]) for g in range(2)]
    qr = [area(f"q_rot{n}", [NP, S]) for n in range(2)]
    sc = area("scores2", [NP, 8, 257])
    pt2 = place("probs2_t", [NP, 16, NP], r_p)
    vb2 = place("v2_t", [NP, 4, NP], r_acc)
    wm = place("window_masks", [NP, 512], r_pad)
    sinkb = place("sinks", [NP, 8], r_st)
    m_sink = load("sinks_and_masks", (sinkb[:, :], sink_in), (wm[:, :], win_in))
    m_pos = load("positions", (posi[:, :], pos_in))
    r0 = copy(V, ang[:, :], posi[:, :], m_pos)
    r1 = ts(V, ang[:, :], ang[:, :], vec("inv_freq"), ALU.mult, None, None, r0)
    TURN, MAGIC = 2 * np.pi, 1.5 * 2 ** 23
    T1 = 6.28125
    T2 = 0.0019350051879882812
    T3 = TURN - T1 - T2
    for dst, quarter in ((sinT, 0.0), (cosT, 0.25)):
        n0 = ts(V, nr[:, :], ang[:, :], 1 / TURN, ALU.mult, quarter, ALU.add, V.now())
        n1 = ts(V, nr[:, :], nr[:, :], MAGIC, ALU.add, None, None, n0)
        n2 = ts(V, nr[:, :], nr[:, :], -MAGIC, ALU.add, None, None, n1)
        n3 = stt(dst[:, :], nr[:, :], -T1, ang[:, :], ALU.mult, ALU.add, n2)
        n4 = stt(dst[:, :], nr[:, :], -T2, dst[:, :], ALU.mult, ALU.add, n3)
        n5 = stt(dst[:, :], nr[:, :], -T3, dst[:, :], ALU.mult, ALU.add, n4)
        n6 = ts(V, dst[:, :], dst[:, :], quarter * TURN, ALU.add, 3.1415925, ALU.min, n5)
        n7 = ts(V, dst[:, :], dst[:, :], -3.1415925, ALU.max, None, None, n6)
        act(dst[:, :], dst[:, :], ACT.Sin, n7)
    trig = A.now()

    rope_free = {}

    def rope(dst, src, b, *after):
        T.need(rope_free.get(b))
        m = T.did(mm(bank[b][:, :], mat("rotate"), src))
        e = tt(G, dst, src, cosT[:, :], ALU.mult, trig, *after)
        d = tt(V, tmp[b % 2][:, :], bank[b][:, :], sinT[:, :], ALU.mult, m, trig, V.now())
        rope_free[b] = d
        return tt(V, dst, dst, tmp[b % 2][:, :], ALU.add, e, d)

    kz = [fill(G, kd[g][:, 0:NP], 0.0) for g in range(2)]
    V.need(r0)
    kr = [rope(kd[g][:, NP:], P[:, KD2 + g, :], 6 + g) for g in range(2)]
    T.need(rope_free[6])
    for n in range(4):
        ins = nc.tensor.transpose(bank[5][:, n * NP:(n + 1) * NP], P[:, V2, n * NP:(n + 1) * NP], mat("ident"))
    m = T.did(ins)
    v2 = copy(A, vb2[:, :, :], bank[5][:, :].rearrange("p (n d) -> p n d", n=4), m)
    stat2 = place("stat2", [NP, 32], r_pb)
    mx, nm, su, rs = (stat2[:, 8 * q:8 * q + 8] for q in range(4))
    maskv = wm[:, :].rearrange("p (a j) -> p a j", a=2)
    G.need(m_sink)
    V.need(m_sink)
    tr_done = None
    out_done = None
    qrot = {}
    qs = place("q_keep", [NP, 4, S], r_opB + 4 * TB)
    qk = copy(G, qs[:, :, :], P[:, 0:4, :])
    T.need(qk)
    for t in range(4):
        g = t // 2
        q0 = rope(qr[t % 2][:, :], qs[:, t, :], 6 + t % 2, T.now(), qk)
        sk = []
        for n in range(4):
            G.need(tr_done, A.now())
            sk.append(copy(G, sc[:, 2 * n:2 * n + 2, 256:257], sinkb[:, 2 * t:2 * t + 2].unsqueeze(2)))
        T.need(q0, kr[g], kz[g])
        ss = []
        for i2 in range(2):
            for q in range(2):
                n = 2 * i2 + q
                for h, (lo, hi) in enumerate(HH):
                    ins = mm(bank[2 * i2 + h][:, q * 256:(q + 1) * 256], qr[t % 2][lo:hi, n * NP:(n + 1) * NP],
                             kd[g][lo:hi, n * NP:n * NP + 256])
            m = T.did(ins)
            mk = maskv if i2 == 0 else maskv[:, 1, :].unsqueeze(1).broadcast_to([NP, 2, 256])
            for h in range(2):
                ss.append(stt(sc[:, 4 * i2 + h:4 * i2 + h + 3:2, 0:256],
                              bank[2 * i2 + h][:, :].rearrange("p (q j) -> p q j", q=2),
                              HD ** -0.5, mk, ALU.mult, ALU.add, m, tr_done))
        V.need(*ss, *sk, A.now())
        x0 = V.did(V.q.reduce_max(mx, sc[:, :, :], AX.X))
        x1_ = ts(V, nm, mx, -1.0, ALU.mult, None, None, x0)
        for e in range(8):
            A.need(x1_)
            ea = A.did(A.q.activation(sc[:, e, :], sc[:, e, :], ACT.Exp, bias=nm[:, e:e + 1], accum_out=su[:, e:e + 1]))
        V.need(ea)
        x2_ = V.did(V.q.reciprocal(rs, su))
        x3_ = tt(V, sc[:, :, 0:256], sc[:, :, 0:256], rs.unsqueeze(2).broadcast_to([NP, 8, 256]), ALU.mult, x2_)
        T.need(x3_)
        pts = []
        for n in range(4):
            for h in range(2):
                for jt in range(2):
                    ins = nc.tensor.transpose(bank[n][:, (2 * h + jt) * NP:(2 * h + jt + 1) * NP],
                                              sc[:, 2 * n + h, jt * NP:(jt + 1) * NP], mat("ident"))
            m = T.did(ins)
            pts.append(copy(A if n % 2 else V, pt2[:, 4 * n:4 * n + 4, :],
                            bank[n][:, :].rearrange("p (a q) -> p a q", a=4), m, out_done, qk))
        tr_done = T.now()
        T.need(*pts, v2, out_done)
        b = 4
        first = [True, True]
        for n in range(4):
            for h, (lo, hi) in enumerate(HH):
                for jt in range(2):
                    if n == 0 and jt == 0:
                        continue
                    ins = mm(bank[b][lo:hi, n * NP:(n + 1) * NP], vb2[:, n - 1 + jt, g * HD:(g + 1) * HD],
                             pt2[:, 4 * n + 2 * h + jt, :], start=first[h], stop=(n == 3 and jt == 1))
                    first[h] = False
        m = T.did(ins)
        ya = tt(V, P[:, ZA + t, :], bank[b][:, :], P[:, ZA + t, :], ALU.mult, m)
        out_done = ya
        two_parts(opB, t, P[:, ZA + t, :], ya)
    if stop == "swa":
        return done(P[:, ZA:ZA + 4, :])

    o = r_opA
    vn = area("v_norm", [NP, 4, HALF])
    lng, lnb, bsb = area("ln_v_g", [NP, HALF]), area("ln_v_b", [NP, HALF]), area("b_s", [NP, 4, NP])
    wsr, wst = area("w_s", [NP, 4, NP]), area("w_s_t", [NP, 4, NP])
    for E in (A, V, G, T):
        E.need(A.now(), V.now(), G.now(), T.now())
    m_sg = load("spatial_gating", (lng[:, :], lnv_in[0]), (lnb[:, :], lnv_in[1]),
                (bsb[:, :, :].rearrange("p g t -> p (g t)"), bs_in), (wsr[:, :, :], ws_in.rearrange("g t s -> t g s")))
    T.need(m_sg)
    V.need(m_sg)
    G.need(m_sg)
    for g in range(4):
        ins = nc.tensor.transpose(bank[4][:, g * NP:(g + 1) * NP], wsr[:, g, :], mat("ident"))
    m = T.did(ins)
    wsd = tt(V, wst[:, :, :], bank[4][:, :].rearrange("p (g t) -> p g t", g=4), wide("causal", 4), ALU.mult, m)
    st6 = place("bn6", [NP, 4, 6], r_st + 64)
    mv = place("bn_mv", [NP, 4, 2], r_st + 256)
    vnd = []
    for n in range(4):
        for q in range(4):
            ins = nc.tensor.transpose(bank[n][:, q * NP:(q + 1) * NP], P[:, VB + q, n * NP:(n + 1) * NP], mat("ident"))
        m = T.did(ins)
        c0 = copy(V, vn[:, n, :], bank[n][:, :], m)
        V.need(c0)
        c1 = V.did(V.q.bn_stats(st6[:, n, :], vn[:, n, :]))
        V.need(c1)
        c2 = V.did(V.q.bn_aggr(mv[:, n, :], st6[:, n, :]))
        c3 = inv_sqrt(mv[:, n, 1:2], mv[:, n, 1:2], 1.0, ALU.add, EPS, c2)
        c4 = ts(V, vn[:, n, :], vn[:, n, :], mv[:, n, 0:1], ALU.subtract, mv[:, n, 1:2], ALU.mult, c3)
        c5 = tt(G, vn[:, n, :], vn[:, n, :], lng[:, :], ALU.mult, c4)
        vnd.append(tt(G, vn[:, n, :], vn[:, n, :], lnb[:, :], ALU.add, c5))
    T.need(*vnd, wsd)
    for g in range(4):
        j = g % 2
        b = 5 + j
        T.need(V.now() if g >= 2 else None)
        for n in range(4):
            ins = mm(bank[b][:, n * NP:(n + 1) * NP], vn[:, n, g * NP:(g + 1) * NP], wst[:, g, :])
        m = T.did(ins)
        e0 = tt(V, tmp[j][:, :].rearrange("p (n t) -> p n t", n=4), bank[b][:, :].rearrange("p (n t) -> p n t", n=4),
                bsb[:, g, :].unsqueeze(1).broadcast_to([NP, 4, NP]), ALU.add, m, V.now(), A.now())
        e1 = tt(V, tmp[j][:, :], tmp[j][:, :], P[:, UB + g, :], ALU.mult, e0)
        e2 = tt(V, tmp[j][:, :], tmp[j][:, :], P[:, ZB + g, :], ALU.mult, e1)
        two_parts(opB, 4 + g, tmp[j][:, :], e2)
    if stop == "y":
        return done(opB[0][:, :, :].bitcast(F32))

    for E in (T, V, A, G):
        E.need(A.now(), V.now(), G.now(), T.now())
    fill(G, acc[:, :], 0.0)
    merged = segment(KT, opB, leave_merge(G2, G2 + 8, opA), two=True, act=1, dve=2, pool=1)

    def leave_final(m, before):
        def leave(ps, freed, out_, j):
            s = act(sq[j][:, :], ps[0], ACT.Square, *before)
            V.need(s)
            freed(V.q.tensor_scalar(tile(P, m), ps[0], gate2v(m), None, ALU.mult))
            tt(G, acc[:, :], acc[:, :], sq[j][:, :], ALU.add, s, G.now())
        return leave

    def gate2v(m):
        return gate2[:, m:m + 1] if isinstance(m, int) else gate2[:, bass.ds(m, 1)]
    segment(KT, opA, leave_final, ready=merged, last=1, act=1, pool=1)
    rms()
    rdone = V.now()
    s_out = nc.alloc_semaphore("stored")
    for k in range(KT):
        E = G if k % 3 == 2 else V
        if k < 3:
            E.wait(s_free, panel_no.n + 2)
        z0 = tt(E, P[:, k, :], P[:, k, :], rstd[:, :], ALU.mult, rdone)
        z1 = tt(E, xT[:, k, :], xT[:, k, :], P[:, k, :], ALU.add, z0)
        nc.sync.wait_ge(z1.sem, z1.value())
        nc.sync.dma_start(out[k * NP:(k + 1) * NP, :], xT[:, k, :]).then_inc(s_out, 16)
    nc.sync.wait_ge(s_out, 16 * KT)
    for E in (T, G):
        nc.sync.wait_ge(E.passed.sem, E.passed.n)
    assert panel_no.n == n_panels, (panel_no.n, n_panels)


WKV_PE, WKV_ACT, WKV_DVE, WKV_POOL = 59, 32, 68, 5


def tiles_of(v):
    return np.asarray(v).reshape(-1, NP).T


def panelled(w):
    k, n = w.shape
    return w.reshape(k // NP, NP, n // NP, NP).transpose(2, 1, 0, 3).reshape(n // NP, NP, k)


def layout(i):
    w_in = i["w_in"][0]
    rw = np.concatenate([w_in[:, 0:1824], np.zeros((D, N_RW * NP - 1824), w_in.dtype)], axis=1)
    rw = panelled(rw)
    rest = panelled(w_in[:, 1824:])
    conv, gates = rest[0:12], rest[12:28]
    mixed = []
    for f in range(FT):
        mixed += [conv[f], conv[4 + f], conv[8 + f], *gates[3 * f:3 * f + 3]]
    mixed += list(gates[12:16])
    proj = panelled(np.concatenate([i["w_proj_a"][0], i["w_proj_b"][0]], axis=0))
    mlp = []
    for c in range(4):
        mlp += [panelled(i["w_up"][0][:, c * D:(c + 1) * D]), panelled(i["w_down"][0][c * D:(c + 1) * D, :])]
    w2 = i["w_in_2"][0]
    o = np.cumsum([0, 512, 128, 128, 512, 512, 512, 512, 2048])
    q, k, v, za, ub, vb, zb, gl = (w2[:, a:b] for a, b in zip(o[:-1], o[1:]))
    k0, k1 = k[:, 0:64], k[:, 64:128]
    in2 = panelled(np.concatenate([q, k0, k0, k1, k1, v, ub, vb, za, zb, gl], axis=1))
    proj2 = panelled(np.concatenate([i["w_proj_a_2"][0], i["w_proj_b_2"][0]], axis=0))
    panels = np.concatenate([rw, np.stack(mixed), proj, panelled(i["w_out_mix"][0]), panelled(i["w_kv"][0]),
                             panelled(i["w_q"][0]), panelled(i["w_xo"][0]), *mlp, in2, proj2,
                             panelled(i["w_out_2"][0])])
    mu = np.concatenate([i["mu_shift"][0], np.zeros(N_RW * NP - 1824, np.float32)])
    half = HD // 2
    freq = (np.float32(10000.0) ** (-np.arange(half, dtype=np.float32) / np.float32(half))).astype(np.float32)
    parts = {
        "norm_mix": i["norm_mix"][0], "b_gate": i["b_gate"][0], "mu": mu, "a0": i["a0"][0],
        "k_k": i["k_k"][0], "k_a": i["k_a"][0], "r_k": i["r_k"][0].reshape(-1), "ln_x_w": i["ln_x_w"][0],
        "ln_x_b": i["ln_x_b"][0], "conv_w": i["conv_w"][0].reshape(-1), "norm_xattn": i["norm_xattn"][0],
        "norm_mem": i["norm_mem"][0], "norm_mlp": i["norm_mlp"][0], "norm_final": i["norm_final"],
        "g_pre": i["g_pre_2"][0], "g_post": i["g_post_2"][0], "b_ada": i["b_ada_2"][0], "c": i["c_2"][0],
        "inv_freq": np.tile(freq, 4),
    }
    vec = np.concatenate([tiles_of(parts[n]) for n, _ in VECS], axis=1)
    lora = np.concatenate([i["w_lora_w"][0], i["w0"][0][None], i["w_lora_a"][0], i["w_lora_g"][0]], axis=0)
    wide = lambda v: np.broadcast_to(np.asarray(v).reshape(1, -1), (NP, np.asarray(v).size))
    arrays = {
        "x": i["x"][0].T, "mem": i["mem"][0].T, "panels": panels, "ada": i["w_ada_2"][0], "vec": vec,
        "mat": constants(), "win": window_masks(), "lora": lora, "pos": wide(i["positions_2"][0]),
        "sink": wide(i["sinks_2"][0]), "ws": i["w_s_2"][0],
        "lnv": np.stack([wide(i["ln_v_g_2"][0]), wide(i["ln_v_b_2"][0])]), "bs": wide(i["b_s_2"][0]),
    }
    return {k: np.ascontiguousarray(v) for k, v in arrays.items()}


STOP, DBG_SHAPE = None, None


def kernel(**inputs):
    import concourse.bacc as bacc
    from concourse.bass_utils import run_bass_kernel_spmd

    nc = bacc.Bacc("TRN2", target_bir_lowering=False, num_devices=1)
    arrays = layout({k: np.asarray(v) for k, v in inputs.items()})
    aps = [nc.dram_tensor(k, v.shape, mybir.dt.from_np(v.dtype), kind="ExternalInput").ap() for k, v in arrays.items()]
    out = nc.dram_tensor("out", DBG_SHAPE or (D, S), F32, kind="ExternalOutput").ap()
    build(nc, *aps, None if STOP else out, stop=STOP, dbg=out)
    r = run_bass_kernel_spmd(nc, [arrays], core_ids=[0])
    got = r.results[0]["out"]
    return got if STOP else np.ascontiguousarray(got.T)[None]
```

```python
import concourse.bass as bass
from concourse import mybir
from concourse.alu_op_type import AluOpType as ALU
import numpy as np

F32, F32R, I32 = mybir.dt.float32, mybir.dt.float32r, mybir.dt.int32
ACT = mybir.ActivationFunctionType
AX = mybir.AxisListType

S = 512
D = 1024
NP = 128
KT = D // NP
N_MEM = 256
HEADS, HD = 8, 64
HALF = D // 2
FT = HALF // NP
L = 64
NC = S // L
XH, XD = 4, 256
EPS = 1e-6
LNX_EPS = 64e-5
DECAY = float(np.exp(np.float32(-0.5)))
NEG = -1e30

N_RW = 15
CONV0 = N_RW
GATE0 = CONV0 + 3 * FT
Q2, KD2, V2, UB, VB, ZA, ZB, G2 = 0, 4, 6, 7, 11, 15, 19, 23
N_IN2 = 39
WKV_PANELS = 6

VECS = [("norm_mix", 8), ("b_gate", 16), ("mu", 15), ("a0", 4), ("k_k", 4), ("k_a", 4), ("r_k", 4),
        ("ln_x_w", 4), ("ln_x_b", 4), ("conv_w", 12), ("norm_xattn", 8), ("norm_mem", 8),
        ("norm_mlp", 8), ("norm_final", 8), ("g_pre", 8), ("g_post", 8), ("b_ada", 24), ("c", 8),
        ("inv_freq", 1)]
COL = {}
_n = 0
for _name, _w in VECS:
    COL[_name] = _n
    _n += _w
N_VEC = _n
LEVELS = [1, 2, 4, 8, 16, 32]
MATS = [("ident", 128), ("mean", 128), ("head_sum", 128), ("cumsum", 128), ("chunk_mask", 128),
        ("rotate", 128), ("causal", 128), ("eye", 64)] + [(f"level{s}", 64) for s in LEVELS]
MAT = {}
_n = 0
for _name, _w in MATS:
    MAT[_name] = (_n, _w)
    _n += _w
N_MAT = _n


def constants():
    i, j = np.arange(128)[:, None], np.arange(128)[None, :]
    j64 = np.arange(64)[None, :]
    same = (i // 64) == (j // 64)
    out = {
        "ident": i == j,
        "mean": np.full((128, 128), 1.0 / D),
        "head_sum": same,
        "cumsum": same & (i <= j),
        "chunk_mask": np.where(j < 64, (i % 64) < (j % 64), (i % 64) <= (j % 64)),
        "rotate": np.where((j % 64) < 32, -1.0 * (i == j + 32), 1.0 * (i == j - 32)),
        "causal": i <= j,
        "eye": (i % 64) == j64,
    }
    for s in LEVELS:
        ii = i % 64
        out[f"level{s}"] = (ii // (2 * s) == j64 // (2 * s)) & ((ii // s) % 2 == 1) & ((j64 // s) % 2 == 0)
    return np.concatenate([out[n].astype(np.float32) for n, _ in MATS], axis=1)


def window_masks():
    q, j = np.arange(128)[:, None], np.arange(256)[None, :]
    rel = q + 128 - j
    ok = (rel >= 0) & (rel < 128)
    first = ok & (j >= 128)
    return np.concatenate([np.where(first, 0.0, NEG), np.where(ok, 0.0, NEG)], axis=1).astype(np.float32)


class Loops:
    running = []


class Mark:

    def __init__(self, counter):
        self.sem, self.n = counter.sem, counter.n
        self.per = [(lo, lo["per"].get(counter.name, 0)) for lo in Loops.running]

    def of_round(self, i):
        m = object.__new__(Mark)
        m.sem, m.n, m.per = self.sem, self.n + i * self.per[-1][1], self.per[:-1]
        return m

    def value(self):
        v = self.n
        for lo, per in self.per:
            assert any(x is lo for x in Loops.running), "a mark of a loop that has ended"
            if per:
                v = lo["i"] * per + v
        return v


class Lane:

    def __init__(self, nc, queue, name):
        self.q, self.name, self.sem, self.n = queue, name, nc.alloc_semaphore("done_" + name), 0
        self.met = {}
        self.passed = Passed(nc, name) if name in ("pe", "pool") else None

    def did(self, ins):
        ins.then_inc(self.sem, 1)
        self.n += 1
        return Mark(self)

    def now(self):
        return Mark(self)

    def ago(self, d):
        m = Mark(self)
        m.n -= d
        return m

    def need(self, *marks):
        for m in marks:
            if m is None or (m.n == 0 and not m.per):
                continue
            key, n = (id(m.sem), *(id(lo) for lo, _ in m.per)), self.met.get(id(m.sem), (None, -1))
            if n[0] == (key, len(Loops.running)) and n[1] >= m.n:
                continue
            self.met[id(m.sem)] = ((key, len(Loops.running)), m.n)
            self.wait(m.sem, m.value())

    def wait(self, sem, value):
        self.q.wait_ge(sem, value)
        if self.passed is not None and not isinstance(value, int):
            self.q.sem_inc(self.passed.sem, 1)
            self.passed.n += 1


class Passed:

    def __init__(self, nc, name):
        self.name, self.sem, self.n = name + "_passed", nc.alloc_semaphore(name + "_waits_passed"), 0


class loop:

    def __init__(self, nc, lanes, count, **per):
        self.nc, self.lanes, self.count, self.per = nc, lanes, count, per

    def __enter__(self):
        lanes = self.lanes
        self.ctx = self.nc.Fori(0, self.count, engines=(
            mybir.EngineType.PE, mybir.EngineType.Activation, mybir.EngineType.DVE, mybir.EngineType.Pool))
        i = self.ctx.__enter__()
        self.entry = {"i": i, "per": self.per}
        self.start = {x.name: x.n for x in lanes}
        self.forget()
        Loops.running.append(self.entry)
        return i

    def forget(self):
        for x in self.lanes:
            if isinstance(x, Lane):
                x.met.clear()

    def __exit__(self, *e):
        self.ctx.__exit__(*e)
        self.forget()
        if e[0] is not None:
            return False
        Loops.running.pop()
        got = {x.name: x.n - self.start[x.name] for x in self.lanes if x.n != self.start[x.name]}
        self.per.update({k: v for k, v in got.items() if k.endswith("_passed")})
        want = {k: v for k, v in self.per.items() if v}
        assert got == want, f"a round raises {got}, not {want}"
        for x in self.lanes:
            x.n = self.start[x.name] + self.count * self.per.get(x.name, 0)
        return False


def tile(t, m):
    if isinstance(m, int):
        return t[:, m, :]
    return t[:, bass.ds(m, 1), :].rearrange("p a n -> p (a n)")


def build(nc, x_in, mem_in, panels, ada_w, vec_in, mat_in, win_in, lora_in, pos_in, sink_in, ws_in,
          lnv_in, bs_in, out):
    T = Lane(nc, nc.tensor, "pe")
    A = Lane(nc, nc.scalar, "act")
    V = Lane(nc, nc.vector, "dve")
    G = Lane(nc, nc.gpsimd, "pool")

    def tt(E, o, a, b, op, *after):
        E.need(*after)
        return E.did(E.q.tensor_tensor(o, a, b, op))

    def ts(E, o, a, s1, op0, s2, op1, *after):
        E.need(*after)
        if op1 is None:
            return E.did(E.q.tensor_scalar(o, a, s1, None, op0))
        return E.did(E.q.tensor_scalar(o, a, s1, s2, op0, op1))

    def stt(o, a, s, b, op0, op1, *after):
        V.need(*after)
        return V.did(V.q.scalar_tensor_tensor(o, a, s, b, op0, op1))

    def act(o, a, f, *after, **kw):
        A.need(*after)
        return A.did(A.q.activation(o, a, f, **kw))

    def copy(E, o, a, *after):
        E.need(*after)
        if E is A:
            return A.did(A.q.activation(o, a, ACT.Copy))
        return E.did(E.q.tensor_copy(o, a))

    def inv_sqrt(dst, src, scale, op, eps, *after):
        m = ts(V, dst, src, scale, ALU.mult, eps, op, *after)
        V.need(act(dst, dst, ACT.Sqrt, m))
        return V.did(V.q.reciprocal(dst, dst))

    def head_inv_sqrt(sq_in, sums_ps, scale, op, eps, *after):
        T.need(*after)
        for q in range(S // NP):
            ins = mm(sums_ps[:, 2 * q:2 * q + 2], sq_in[:, q * NP:(q + 1) * NP], mat("head_sum")[:, 0:NP:HD])
        m = ts(V, head_cols, sums_ps[:, 0:2 * S // NP], scale, ALU.mult, eps, op, T.did(ins))
        V.need(act(head_cols, head_cols, ACT.Sqrt, m))
        m = V.did(V.q.reciprocal(head_cols, head_cols))
        m = copy(V, sq_in[:, :].rearrange("p (q h) -> p q h", h=HD),
                 head_cols.unsqueeze(2).broadcast_to([NP, 2 * S // NP, HD]), m)
        return m

    def head_spread(src, out_ps, *after):
        T.need(*after)
        for q in range(S // NP):
            ins = nc.tensor.transpose(out_ps[:, q * NP:(q + 1) * NP], src[:, q * NP:(q + 1) * NP], mat("ident"))
        return T.did(ins)

    def fill(E, o, v, *after):
        E.need(*after)
        return E.did(E.q.memset(o, v))

    def mm(o, lhsT, rhs, start=True, stop=True):
        return nc.tensor.matmul(o, lhsT, rhs, start=start, stop=stop, skip_group_check=True)

    at = [(nc.sbuf_base + 31) // 32 * 32]

    def region(nbytes):
        a = at[0]
        at[0] += (nbytes + 31) // 32 * 32
        assert at[0] <= nc.sbuf_usable_end, f"sbuf {at[0]}"
        return a

    def place(name, shape, offset, dt=F32):
        return nc.alloc_sbuf_tensor_at(name, shape, dt, offset=offset)

    TB = S * 4
    r_x, r_opA, r_opB = region(KT * TB), region(2 * KT * TB), region(2 * KT * TB + 32)
    r_w = region(6 * KT * NP * 4)
    r_p = region(N_IN2 * TB)
    r_rstd, r_pad, r_tmp, r_sq, r_acc = region(TB), region(2 * (S + 8) * 4), region(2 * TB), region(2 * TB), region(TB)
    r_mat, r_vec = region(N_MAT * 4), region(N_VEC * 4)
    r_col = region(64 * 4)
    r_pb, r_st = region(NC * (L + 1) * 4), region(3 * L * 4)

    xT = place("xT", [NP, KT, S], r_x)
    opA = [place(f"opA_{p}", [NP, KT, S], r_opA + n * KT * TB, F32R) for n, p in enumerate(("hi", "lo"))]
    opB = [place(f"opB_{p}", [NP, KT, S], r_opB + n * KT * TB, F32R) for n, p in enumerate(("hi", "lo"))]
    WB = KT * NP * 4
    w_raw = place("w_raw", [NP, 2, KT * NP], r_w)
    w_hi = [place(f"w_hi{j}", [NP, KT, NP], r_w + (2 + j) * WB, F32R) for j in range(2)]
    w_lo = [place(f"w_lo{j}", [NP, KT, NP], r_w + (4 + j) * WB, F32R) for j in range(2)]
    P = place("P", [NP, N_IN2, S], r_p)
    rstd = place("rstd", [NP, S], r_rstd)
    pad = [place(f"pad{j}", [NP, S + 2], r_pad + j * (S + 8) * 4) for j in range(2)]
    tmp = [place(f"tmp{j}", [NP, S], r_tmp + j * TB) for j in range(2)]
    sq = [place(f"sq{j}", [NP, S], r_sq + j * TB) for j in range(2)]
    acc = place("acc", [NP, S], r_acc)
    acc2, r1 = place("acc2", [NP, S], r_pad), place("rstd_first", [NP, S], r_pad + TB)
    mats = place("mats", [NP, N_MAT], r_mat)
    vecs = place("vecs", [NP, N_VEC], r_vec)
    cols = place("cols", [NP, 64], r_col)
    adac, gain2, gate2, silc, gain3 = (cols[:, a:b] for a, b in ((0, 24), (24, 32), (32, 40), (40, 48), (48, 56)))
    head_cols = cols[:, 56:56 + 2 * S // NP]

    def mat(name):
        a, w = MAT[name]
        return mats[:, a:a + w]

    def vec(name, m=0):
        c = m + COL[name]
        return vecs[:, c:c + 1] if isinstance(c, int) else vecs[:, bass.ds(c, 1)]

    bank = [nc.alloc_psum_tensor(f"bank{b}", [NP, S], F32) for b in range(8)]

    def load(name, *pairs, queue=nc.scalar):
        class arrived:
            sem, n = nc.alloc_semaphore("loaded_" + name), 16 * len(pairs)
        arrived.name = name
        for o, i in pairs:
            queue.dma_start(o, i).then_inc(arrived.sem, 16)
        return Mark(arrived)

    def tiled(ap):
        return ap.rearrange("(k p) n -> p k n", p=NP)

    m_const = load("constants", (vecs[:, :], vec_in), (mats[:, :], mat_in))
    m_x = [load(f"x{q}", (xT[:, 2 * q:2 * q + 2, :], tiled(x_in)[:, 2 * q:2 * q + 2, :]),
                queue=(nc.scalar, nc.gpsimd)[q % 2]) for q in range(4)]
    lw = place("lora_w", [65, HALF], r_p + 15 * TB)
    la = place("lora_a", [NP, HALF], r_p + 16 * TB)
    lg = [place("lora_g0", [NP, HALF], r_p + 17 * TB), place("lora_g1", [32, HALF], r_p + 18 * TB)]
    m_lora = load("lora", (lw[:, :], lora_in[0:65, :]), (la[64:128, :], lora_in[65:129, :]),
                  (lg[0][:, :], lora_in[129:257, :]), (lg[1][:, :], lora_in[257:289, :]))

    s_raw = [nc.alloc_semaphore(f"raw_panel_in_slot{j}") for j in range(2)]
    s_hi, s_lo = nc.alloc_semaphore("high_parts_made"), nc.alloc_semaphore("low_parts_made")
    s_mm, s_free = nc.alloc_semaphore("panels_multiplied"), nc.alloc_semaphore("banks_freed")
    nc.vector.sem_inc(s_lo, 2)
    nc.vector.sem_inc(s_free, 2)
    nc.tensor.sem_inc(s_mm, 2)
    n_panels = panels.shape[0]

    class panel_no:
        name, n = "panels", 0
    lanes = [T, A, V, G, panel_no, T.passed, G.passed]

    def panel_value(ahead=0, half=False):
        v = panel_no.n + ahead
        v = v // 2 if half else v
        for lo in Loops.running:
            per = lo["per"].get("panels", 0)
            assert per % 2 == 0
            if per:
                v = lo["i"] * (per // 2 if half else per) + v
        return v

    with nc.sync.Fori(0, n_panels // 2) as h:
        for j in range(2):
            nc.sync.wait_ge(s_lo, h * 2 + (j + 1))
            nc.sync.dma_start(w_raw[:, j, :],
                              panels[bass.ds(h * 2 + j, 1), :, :].rearrange("a p n -> p (a n)")).then_inc(s_raw[j], 16)

    def split(ahead):
        j = (panel_no.n + ahead) % 2
        flat = "p k n -> p (k n)"
        A.q.wait_ge(s_raw[j], panel_value(ahead, half=True) * 16 + 16)
        A.q.wait_ge(s_mm, panel_value(ahead) + 1)
        A.q.activation(w_hi[j][:, :, :].rearrange(flat), w_raw[:, j, :], ACT.Copy).then_inc(s_hi, 1)
        V.q.wait_ge(s_hi, panel_value(ahead) + 1)
        V.q.tensor_tensor(w_lo[j][:, :, :].rearrange(flat), w_raw[:, j, :],
                          w_hi[j][:, :, :].rearrange(flat).bitcast(F32), ALU.subtract).then_inc(s_lo, 1)

    def panel(op, leave, n=S, two=False, last=False, ready=None, between=None):
        steps = panel_steps(op, leave, n, two, last, ready, between)
        for made in steps:
            pass
        return made

    def panel_steps(op, leave, n=S, two=False, last=False, ready=None, between=None):
        j = panel_no.n % 2
        T.q.wait_ge(s_lo, panel_value() + 3)
        T.q.wait_ge(s_free, panel_value() + 1)
        hi, lo = op
        ps = [bank[j], bank[2 + j]] if two else [bank[j]]
        if not last:
            split(1)
        for k in range(KT):
            if ready:
                T.need(ready[k])
            o = ps[k // (KT // 2) if two else 0][:, 0:n]
            first, end = k % (KT // 2 if two else KT) == 0, (k + 1) % (KT // 2 if two else KT) == 0
            nc.tensor.matmul(o, w_hi[j][:, k, :], hi[:, k, 0:n], start=first, stop=False)
            nc.tensor.matmul(o, w_hi[j][:, k, :], lo[:, k, 0:n], start=False, stop=False)
            ins = nc.tensor.matmul(o, w_lo[j][:, k, :], hi[:, k, 0:n], start=False, stop=end)
            if k < KT - 1:
                yield None
        ins.then_inc(s_mm, 1)
        if between:
            between()
        V.q.wait_ge(s_mm, panel_value() + 3)
        A.q.wait_ge(s_mm, panel_value() + 3)

        def freed(ins):
            ins.then_inc(s_free, 1)

        def out_of_psum(E):
            E.wait(s_free, panel_value() + 3)

        made = leave([p[:, 0:n] for p in ps], freed, out_of_psum, j)
        panel_no.n += 1
        yield made

    def segment(count, op, make, n=S, two=False, last=0, ready=None, between=None, **per):
        made = []

        def some(ms, **kw):
            before = [A.now(), V.now(), G.now()]
            for m in ms:
                made.append(panel(op, make(m, before), n=n, two=two, **kw))
                kw.pop("between", None)

        first = 2 if ready or between else 0
        if first:
            some(range(2), ready=ready, between=between)
        pairs = (count - first) // 2 - (1 if last else 0)
        if pairs > 0:
            with loop(nc, lanes, pairs, panels=2, **{k: 2 * v for k, v in per.items()}) as i:
                some([i * 2 + (j + first) for j in range(2)])
            round_marks = [made.pop() for _ in range(2)][::-1]
            made += [m and m.of_round(i) for i in range(pairs) for m in round_marks]
        if last:
            some([count - 2])
            some([count - 1], last=True)
        elif count % 2:
            some([count - 1])
        return made

    def leave_plain(dst, scale_by, base=0):
        def make(m, before):
            def leave(ps, freed, out, j):
                freed(V.q.tensor_tensor(tile(dst, m + base), ps[0], scale_by, ALU.mult))
            return leave
        return make

    def leave_copy(base):
        def make(m, before):
            def leave(ps, freed, out, j):
                freed(V.q.tensor_copy(tile(P, m + base), ps[0]))
            return leave
        return make

    def scaled(ps, freed, out, j, before):
        V.need(*before)
        freed(V.q.tensor_tensor(tmp[j][:, :], ps[0], rstd[:, :], ALU.mult))

    def leave_function(base, f):
        def make(m, before):
            def leave(ps, freed, out, j):
                freed(A.q.activation(tile(P, m + base), ps[0], f))
            return leave
        return make

    def leave_silu(base):
        def make(m, before):
            def leave(ps, freed, out, j):
                V.need(act(tmp[j][:, :], ps[0], ACT.Sigmoid, *before))
                freed(V.q.tensor_tensor(tile(P, m + base), ps[0], tmp[j][:, :], ALU.mult))
            return leave
        return make

    def leave_shift(base):
        def make(m, before):
            def leave(ps, freed, out, j):
                V.need(*before)
                freed(V.q.tensor_tensor(pad[j][:, 1:S + 1], ps[0], rstd[:, :], ALU.mult))
                out(G)
                d = tt(G, tmp[j][:, :], pad[j][:, 0:S], pad[j][:, 1:S + 1], ALU.subtract)
                stt(tile(P, m + base), tmp[j][:, :], vec("mu", m), pad[j][:, 1:S + 1], ALU.mult, ALU.add, d)
            return leave
        return make

    def square_sum(src, j, gain, op, m, *after, n=S):
        h = act(tile(op[0], m)[:, 0:n], src, ACT.Copy, *after, scale=gain)
        lo = stt(tile(op[1], m)[:, 0:n], src, gain, tile(op[0], m)[:, 0:n].bitcast(F32), ALU.mult, ALU.subtract, h)
        s = act(sq[j][:, 0:n], src, ACT.Square)
        tt(G, acc[:, 0:n], acc[:, 0:n], sq[j][:, 0:n], ALU.add, s, G.now())
        return lo

    def leave_residual(gain=None, op=None):
        def make(m, before):
            def leave(ps, freed, out, j):
                freed(V.q.tensor_tensor(tile(xT, m), ps[0], tile(xT, m), ALU.add))
                if gain:
                    out(A)
                    out(V)
                    return square_sum(tile(xT, m), j, vec(gain, m), op, m, *before)
            return leave
        return make

    def rms(eps=EPS, n=S, dst=rstd, sums=(acc,), clear=True):
        T.need(G.now())
        for i, a in enumerate(sums):
            ins = mm(bank[7][:, 0:n], mat("mean"), a[:, 0:n], i == 0, i == len(sums) - 1)
        m = T.did(ins)
        r = inv_sqrt(dst[:, 0:n], bank[7][:, 0:n], 1.0, ALU.add, eps, m)
        if clear:
            fill(G, acc[:, :], 0.0, m)
        V.need(r)

    def token_cols(sums, dst):
        for q in range(S // NP):
            ins = mm(dst[:, q:q + 1], sums[:, q * NP:(q + 1) * NP], mat("mean")[:, 0:1])
        return T.did(ins)

    def token_wide(cols_, wide_, ps, *after):
        m = copy(V, wide_[:, :].rearrange("p (q i) -> p q i", i=NP), cols_.unsqueeze(2).broadcast_to([NP, S // NP, NP]), *after)
        T.need(m)
        for q in range(S // NP):
            ins = nc.tensor.transpose(ps[:, q * NP:(q + 1) * NP], wide_[:, q * NP:(q + 1) * NP], mat("ident"))
        return T.did(ins)

    def two_parts(op, m, src, *after):
        h = act(tile(op[0], m), src, ACT.Copy, *after)
        return tt(V, tile(op[1], m), src, tile(op[0], m).bitcast(F32), ALU.subtract, h, *after)

    fill(G, acc[:, :], 0.0)
    fill(G, pad[0][:, 0:1], 0.0)
    fill(G, pad[1][:, 0:1], 0.0)
    for E in (T, A, V, G):
        E.need(m_const)
    split(0)
    ready = []
    for k in range(KT):
        x = xT[:, k, :]
        h = act(opA[0][:, k, :], x, ACT.Copy, m_x[k // 2], scale=vec("norm_mix", k))
        ready.append(stt(opA[1][:, k, :], x, vec("norm_mix", k), opA[0][:, k, :].bitcast(F32), ALU.mult,
                         ALU.subtract, m_x[k // 2], h))

    def first_rms():
        s0 = GATE0 + 4
        for k in [0, 5, 1, 2, 6, 3, 7, 4]:
            q = act(P[:, s0 + k, :], xT[:, k, :], ACT.Square)
            if k not in (0, 5):
                E, to = (V, s0) if k < 5 else (G, s0 + 5)
                tt(E, P[:, to, :], P[:, to, :], P[:, s0 + k, :], ALU.add, q, E.now())
        T.need(V.now())
        rms(sums=(P[:, s0, :], P[:, s0 + 5, :]))

    segment(N_RW, opA, leave_shift(0), pool=1, dve=1, ready=ready, between=first_rms)

    r_sg, r_cum, r_a, r_g = (r_opB + n * FT * TB for n in range(4))
    sg = place("decay_sigmoid", [NP, FT, HALF], r_sg)
    cum = place("decay_sums", [NP, FT, S], r_cum)
    aa = place("a", [NP, FT, S], r_a)
    gg = place("g", [NP, FT, S], r_g)
    th = place("tanh_wd", [65, S], r_p + 19 * TB)
    fill(V, th[64:65, :], 1.0)
    t1 = act(th[0:64, :], P[0:64, 12, :], ACT.Tanh, V.now())
    t2 = act(P[:, 13, :], P[:, 13, :], ACT.Sigmoid, V.now())
    act(P[0:32, 14, :], P[0:32, 14, :], ACT.Sigmoid)
    T.need(m_lora, A.now(), G.now(), V.now())
    free = {}
    for t in range(FT):
        b = 2 + t % 2
        T.need(free.get(b))
        m = T.did(mm(bank[b][:, :], th[:, t * NP:(t + 1) * NP], lw[:, :]))
        free[b] = act(sg[:, t, :], bank[b][:, :], ACT.Sigmoid, m)
    for f in range(FT):
        b = 4 + f % 2
        T.need(free.get(b))
        m = T.did(mm(bank[b][:, :], la[64:128, f * NP:(f + 1) * NP], P[64:128, 12, :]))
        free[b] = act(aa[:, f, :], bank[b][:, :], ACT.Sigmoid, m, bias=vec("a0", f))
    for f in range(FT):
        b = 6 + f % 2
        T.need(free.get(b))
        mm(bank[b][:, :], lg[0][:, f * NP:(f + 1) * NP], P[:, 13, :], True, False)
        m = T.did(mm(bank[b][:, :], lg[1][:, f * NP:(f + 1) * NP], P[0:32, 14, :], False, True))
        free[b] = copy(V, gg[:, f, :], bank[b][:, :], m)
    for f in range(FT):
        b = 2 + f % 2
        T.need(free.get(b), A.now())
        for t in range(FT):
            m = mm(bank[b][:, t * NP:(t + 1) * NP], sg[:, t, f * NP:(f + 1) * NP], mat("cumsum"))
        m = T.did(m)
        free[b] = copy(V, cum[:, f, :], bank[b][:, :], m)

    AR = place("AR", [NP, NC, 2 * L], r_x)
    BKt = place("BK_t", [NP, NC, NP], r_x + 4096)
    GT = place("GT", [NP, NC, 2, 2 * L], r_x + 8192)
    w4 = [place(f"work{n}", [NP, S], r_x + 8192 + n * TB) for n in range(4)]
    BK = place("BK", [NP, NC, 2 * L], r_sg)
    At = place("A_t", [NP, NC, L], r_sg)
    UV = place("UV", [NP, NC, NP], r_sg + 4096)
    X = place("X", [NP, NC, L], r_p + 12 * TB)
    XT = place("XT", [NP, NC, L], r_p + 13 * TB)
    Y = place("Y", [NP, NC, L], r_p + 14 * TB)
    Z = place("Z", [NP, NC, L], r_pad)
    WT = place("WT", [NP, NC, L], r_pad + TB)
    ABT = place("ABT", [NP, NC, L], r_sq)
    y, ysq = place("y", [NP, S], r_p + 12 * TB), place("y_squared", [NP, S], r_p + 13 * TB)
    vs = place("v_copy", [NP, S], r_sq + TB)
    Pb = place("P_chunk", [NP, NC, L + 1], r_pb)
    st = [place(f"state{n}", [NP, L], r_st + n * L * 4) for n in range(2)]
    st_p = place("state_decayed", [NP, L], r_st + 2 * L * 4)
    HH = [(0, 64), (64, 128)]
    C8 = "p (c l) -> p c l"

    def c8(ap):
        return ap.rearrange(C8, c=NC)

    def wide(name, n):
        a, w = MAT[name]
        return mats[:, a:a + w].unsqueeze(1).broadcast_to([NP, n, w])

    fill(G, Pb[:, :, 0:1], 1.0)
    for E in (T, A, V, G):
        E.need(A.now(), V.now(), G.now())

    counts = dict(pe=WKV_PE, act=WKV_ACT, dve=WKV_DVE, pool=WKV_POOL)
    with loop(nc, lanes, FT, panels=WKV_PANELS, **counts) as f:
        start = [T.now(), A.ago(1), V.now(), G.ago(2)]
        rt, kt, vt = tile(P, f), tile(P, f + 4), tile(P, f + 8)
        at_, ct = tile(aa, f), tile(cum, f)
        pieces = []

        def filler_panel(e):
            before = [A.now(), V.now(), G.now()]
            if e < 3:
                return panel_steps(opA, leave_plain(P, rstd[:, :])(f * 3 + (CONV0 + e), before))
            m = f * 3 + (e - 3)

            def step(ps, freed, out_, j):
                scaled(ps, freed, out_, j, before)
                out_(A)
                A.did(A.q.activation(tile(P, m + GATE0), tmp[j][:, :], ACT.Sigmoid, bias=vec("b_gate", m)))
            return panel_steps(opA, step)

        def filler(count=1):
            for _ in range(count):
                e, k = divmod(len(pieces), KT)
                if e < WKV_PANELS:
                    steps = filler_panel(e) if k == 0 else pieces[-1]
                    next(steps)
                    pieces.append(steps)

        kk, t_b, kp, pinv = w4
        for E in (A, V, G):
            E.need(*start)
        k1 = ts(V, kk[:, :], kt, vec("k_k", f), ALU.mult, None, None)
        k2 = tt(V, t_b[:, :], kk[:, :], kk[:, :], ALU.mult, k1)
        p1 = act(Pb[:, :, 1:L + 1], c8(ct), ACT.Exp, scale=-DECAY)
        p2 = act(pinv[:, :], ct, ACT.Exp, scale=DECAY)
        filler(F_START)
        T.need(*start)
        b1 = tt(G, BK[:, :, 0:L], c8(kk[:, :]), c8(at_), ALU.mult, k1)
        n3 = head_inv_sqrt(t_b, bank[2], 1.0, ALU.max, 1e-24, k2)
        ar1 = stt(AR[:, :, 0:L], c8(kk[:, :]), -1.0, Pb[:, :, 0:L], ALU.mult, ALU.mult, k1, p1)
        kp1 = ts(V, kp[:, :], at_, -1.0, ALU.add, vec("k_a", f), ALU.mult)
        b2 = tt(G, BK[:, :, 0:L], BK[:, :, 0:L], c8(pinv[:, :]), ALU.mult, b1, p2)
        filler(F_NORM)
        n4 = head_spread(t_b, bank[3], n3)
        ar1 = tt(V, AR[:, :, 0:L], AR[:, :, 0:L], c8(bank[3][:, :]), ALU.mult, n4, ar1)
        b2 = tt(V, BK[:, :, 0:L], BK[:, :, 0:L], c8(bank[3][:, :]), ALU.mult, b2)
        ar2 = tt(G, AR[:, :, L:2 * L], c8(rt), Pb[:, :, 1:L + 1], ALU.mult, p1)
        kp2 = stt(kp[:, :], kp[:, :], 1.0, kt, ALU.add, ALU.mult, kp1)
        b3 = tt(V, BK[:, :, L:2 * L], c8(kp[:, :]), c8(pinv[:, :]), ALU.mult, kp2, p2)
        vcopy = copy(G, vs[:, :], vt)
        bo1 = stt(t_b[:, :], rt, vec("r_k", f), kp[:, :], ALU.mult, ALU.mult, n4)
        filler(F_AB)

        T.need(ar1, b2)
        for dst, left, right in ((3, AR, BK), (4, BK, AR)):
            for c in range(NC):
                for h, (lo, hi) in enumerate(HH):
                    ins = mm(bank[dst][lo:hi, c * L:(c + 1) * L], left[lo:hi, c, 0:L], right[lo:hi, c, 0:L])
            m = T.did(ins)
            if dst == 3:
                x1 = tt(V, X[:, :, :], c8(bank[3][:, :]), wide("level1", NC), ALU.mult, m)
                x2 = tt(V, X[:, :, :], X[:, :, :], wide("eye", NC), ALU.add, x1)
            else:
                abt = copy(A, ABT[:, :, :], c8(bank[4][:, :]), m)
        filler(F_X)
        T.need(x2)
        for c in range(NC):
            for lo, hi in HH:
                ins = mm(bank[5][lo:hi, c * L:(c + 1) * L], X[lo:hi, c, :], mat("ident")[lo:hi, lo:hi])
        m = T.did(ins)
        xt = copy(A, XT[:, :, :], c8(bank[5][:, :]), m)
        T.need(bo1)
        bo2 = T.did(mm(bank[2][:, :], mat("head_sum"), t_b[:, :]))
        bo3 = tt(V, rt, bank[2][:, :], vt, ALU.mult, bo2, ar2)
        T.need(ar2, b3)
        g_free = {6: V.now(), 7: V.now(), 2: bo3, 3: x1}
        for r in range(2):
            bb = ((6, 7), (2, 3))[r]
            T.need(g_free[bb[0]], g_free[bb[1]])
            for q in range(4):
                for h, (lo, hi) in enumerate(HH):
                    ins = mm(bank[bb[h]][:, q * NP:(q + 1) * NP], BK[lo:hi, 4 * r + q, :], AR[lo:hi, 4 * r + q, :])
            m = T.did(ins)
            V.need(bo3, b3)
            for h in range(2):
                gt = tt(V, GT[:, 4 * r:4 * r + 4, h, :], bank[bb[h]][:, :].rearrange("p (a l) -> p a l", a=4),
                        wide("chunk_mask", 4), ALU.mult, m)
                g_free[bb[h]] = gt
        g_free[5] = xt
        g_free[4] = abt
        bt = []
        for r in range(2):
            b = (5, 4)[r]
            T.need(g_free[b])
            for q in range(4):
                ins = nc.tensor.transpose(bank[b][:, q * NP:(q + 1) * NP], BK[:, 4 * r + q, :], mat("ident"))
            m = T.did(ins)
            g_free[b] = copy(A, BKt[:, 4 * r:4 * r + 4, :], bank[b][:, :].rearrange("p (a l) -> p a l", a=4), m)
        bkt = g_free[4]
        for r in range(2):
            b = (6, 7)[r]
            T.need(g_free[b], vcopy)
            for q in range(4):
                c = 4 * r + q
                ins = mm(bank[b][64:128, q * NP:(q + 1) * NP], vs[:, c * L:(c + 1) * L], mat("ident"))
            m = T.did(ins)
            g_free[b] = copy(A, UV[64:128, 4 * r:4 * r + 4, :],
                             bank[b][64:128, :].rearrange("p (a l) -> p a l", a=4), m)
        uv = g_free[7]
        T.need(g_free[2])
        for c in range(NC):
            for lo, hi in HH:
                ins = mm(bank[2][lo:hi, c * L:(c + 1) * L], AR[lo:hi, c, 0:L], mat("ident")[lo:hi, lo:hi])
        m = T.did(ins)
        at_m = g_free[2] = copy(V, At[:, :, :], c8(bank[2][:, :]), m)

        xd = {0: [x2, xt, abt], 1: [x2, xt, abt]}
        yb_free = {0: [g_free[2], g_free[3]], 1: [g_free[4], g_free[5]]}
        for s in LEVELS[1:]:
            lastl = s == LEVELS[-1]
            ym = {}
            filler(F_SOLVE)
            for g in range(2):
                cs, b = range(4 * g, 4 * g + 4), 2 + 2 * g
                T.need(*xd[g], *yb_free[g])
                for n, c in enumerate(cs):
                    for lo, hi in HH:
                        ins = mm(bank[b][lo:hi, n * L:(n + 1) * L], ABT[lo:hi, c, :], X[lo:hi, c, :])
                m = T.did(ins)
                ym[g] = tt(V, Y[:, 4 * g:4 * g + 4, :], bank[b][:, 0:4 * L].rearrange("p (c l) -> p c l", c=4),
                           wide(f"level{s}", 4), ALU.mult, m)
            filler(F_SOLVE)
            for g in range(2):
                cs, b = range(4 * g, 4 * g + 4), 3 + 2 * g
                T.need(ym[g])
                if not lastl:
                    for n, c in enumerate(cs):
                        for lo, hi in HH:
                            mm(bank[b][lo:hi, n * L:(n + 1) * L], XT[lo:hi, c, :], Y[lo:hi, c, :])
                for n, c in enumerate(cs):
                    for lo, hi in HH:
                        ins = mm(bank[b][lo:hi, (4 + n) * L:(5 + n) * L], Y[lo:hi, c, :], XT[lo:hi, c, :])
                m = T.did(ins)
                dst = slice(4 * g, 4 * g + 4)
                d = [tt(V, XT[:, dst, :], XT[:, dst, :],
                        bank[b][:, 4 * L:8 * L].rearrange("p (c l) -> p c l", c=4), ALU.add, m)]
                if not lastl:
                    d.append(tt(V, X[:, dst, :], X[:, dst, :],
                                bank[b][:, 0:4 * L].rearrange("p (c l) -> p c l", c=4), ALU.add, m))
                xd[g] = d
                yb_free[g] = d
        T.need(uv, gt, *xd[0], *xd[1], at_m, bkt)
        for c in range(NC):
            for h, (lo, hi) in enumerate(HH):
                ins = mm(bank[6][lo:hi, c * L:(c + 1) * L], GT[64:128, c, h, 0:L], UV[64:128, c, lo:hi])
        m = T.did(ins)
        z = copy(V, Z[:, :, :], c8(bank[6][:, :]), m)
        for c in range(NC):
            for h, (lo, hi) in enumerate(HH):
                ins = mm(bank[7][lo:hi, c * L:(c + 1) * L], At[lo:hi, c, :], XT[lo:hi, c, :])
        m = T.did(ins)
        wt = copy(A, WT[:, :, :], c8(bank[7][:, :]), m)

        s0 = fill(G, st[0][:, :], 0.0)
        sready, s_free_b = s0, {4: None, 5: None}
        u = []
        T.need(z, wt, g_free[6])
        for c in range(NC):
            bs = 4 + c % 2
            T.need(*u)
            for h, (lo, hi) in enumerate(HH):
                mm(bank[2 + h][0:L, 0:L], XT[lo:hi, c, :], Z[lo:hi, c, :], True, False)
            T.need(sready)
            for h, (lo, hi) in enumerate(HH):
                ins = mm(bank[2 + h][0:L, 0:L], WT[lo:hi, c, :], st[c % 2][lo:hi, :], False, True)
            m = T.did(ins)
            u = [copy((A, V)[h], UV[0:L, c, lo:hi], bank[2 + h][0:L, 0:L], m) for h, (lo, hi) in enumerate(HH)]
            if c < NC - 1:
                sp = act(st_p[:, :], st[c % 2][:, :], ACT.Copy, sready, V.now(), scale=Pb[:, c, L:L + 1])
            filler(F_CHAIN)
            if c < NC - 1:
                T.need(*u, s_free_b[bs])
                for h, (lo, hi) in enumerate(HH):
                    ins = mm(bank[bs][lo:hi, 0:L], BKt[:, c, lo:hi], UV[:, c, lo:hi])
                m = T.did(ins)
                V.need(T.now())
            else:
                T.need(*u)
            for h, (lo, hi) in enumerate(HH):
                mm(bank[6][lo:hi, c * L:(c + 1) * L], st[c % 2][lo:hi, :], AR[lo:hi, c, L:2 * L], start=(c == 0), stop=False)
            for h, (lo, hi) in enumerate(HH):
                ins = mm(bank[6][lo:hi, c * L:(c + 1) * L], UV[:, c, lo:hi], GT[:, c, h, L:2 * L], start=False,
                         stop=(c == NC - 1))
            ym_ = T.did(ins)
            if c < NC - 1:
                sready = stt(st[1 - c % 2][:, :], bank[bs][:, 0:L], Pb[:, c, L:L + 1], st_p[:, :],
                             ALU.mult, ALU.add, m, sp)
                s_free_b[bs] = sready
            filler(F_CHAIN)

        y1 = copy(A, y[:, :], bank[6][:, :], ym_)
        filler(1)
        T.need(y1)
        m = T.did(mm(bank[2][:, :], mat("head_sum"), y[:, :]))
        y2 = stt(y[:, :], bank[2][:, :], -1.0 / HD, y[:, :], ALU.mult, ALU.add, m)
        y3 = tt(V, ysq[:, :], y[:, :], y[:, :], ALU.mult, y2)
        filler(F_TAIL)
        y5 = head_inv_sqrt(ysq, bank[3], 1.0 / HD, ALU.add, LNX_EPS, y3)
        filler(F_TAIL2)
        m = head_spread(ysq, bank[4], y5)
        y6 = tt(V, y[:, :], y[:, :], bank[4][:, :], ALU.mult, m)
        y7 = act(y[:, :], y[:, :], ACT.Identity, y6, scale=vec("ln_x_w", f), bias=vec("ln_x_b", f))
        y8 = tt(G, y[:, :], y[:, :], rt, ALU.add, y7, bo3)
        y9 = tt(G, tile(gg, f), tile(gg, f), y[:, :], ALU.mult, y8)
        filler(KT * WKV_PANELS - len(pieces))

    A.need(V.now(), T.now())
    m_x = load("x_again", (xT[:, :, :], tiled(x_in)))
    memT = place("memT", [NP, KT, N_MEM], r_p + 4 * TB)
    memo = [place(f"mem_{p}", [NP, KT, N_MEM], r_p + (8 + 4 * n) * TB, F32R) for n, p in enumerate(("hi", "lo"))]
    kvT = place("kvT", [NP, 2 * KT, N_MEM], r_p + 16 * TB)
    vtm = place("v_mem", [NP, 2, D], r_p)
    qT = place("qT", [NP, KT, S], r_p + 24 * TB)
    rstd_m = place("rstd_mem", [NP, N_MEM], r_pad)
    A.need(G.now())
    m_mem = load("mem", (memT[:, :, :], tiled(mem_in)))
    fill(V, pad[0][:, 0:2], 0.0, A.now(), V.now(), T.now(), G.now())
    fill(V, pad[1][:, 0:2], 0.0)
    for f in range(FT):
        m = 3 * FT + f

        def step(ps, freed, out_, j, m=m, f=f):
            scaled(ps, freed, out_, j, [A.now(), V.now()])
            out_(A)
            A.did(A.q.activation(P[:, m - 3 * FT, :], tmp[j][:, :], ACT.Sigmoid, bias=vec("b_gate", m)))
            u = pad[j]
            cb, cc, cx = (P[:, CONV0 + 3 * f + n, :] for n in range(3))
            c0 = tt(V, u[:, 2:S + 2], cc, cx, ALU.mult, V.now())
            c1 = ts(V, cc, u[:, 0:S], vec("conv_w", f), ALU.mult, None, None, c0)
            c2 = stt(cc, u[:, 1:S + 1], vec("conv_w", 4 + f), cc, ALU.mult, ALU.add, c1)
            c3 = stt(cc, u[:, 2:S + 2], vec("conv_w", 8 + f), cc, ALU.mult, ALU.add, c2)
            tt(V, cb, cb, cc, ALU.mult, c3)
        panel(opA, step)

    A.q.wait_ge(s_mm, panel_no.n + 2)
    V.q.wait_ge(s_mm, panel_no.n + 2)
    A.need(V.now())
    ready = [two_parts(opA, f, gg[:, f, :]) for f in range(FT)]
    ready += [two_parts(opA, 4 + f, P[:, CONV0 + 3 * f, :]) for f in range(FT)]

    mem_sum = place("mem_square_sum", [NP, N_MEM], r_pad + TB)
    mem_sq = [place(f"mem_square{j}", [NP, N_MEM], (r_rstd, r_pb)[j // 2] + j % 2 * N_MEM * 4) for j in range(4)]

    def memory_parts(ms):
        A.need(m_mem, V.now(), G.now())
        V.need(m_mem, A.now())
        for m in ms:
            h = act(memo[0][:, m, :], memT[:, m, :], ACT.Copy, scale=vec("norm_mem", m))
            stt(memo[1][:, m, :], memT[:, m, :], vec("norm_mem", m), memo[0][:, m, :].bitcast(F32), ALU.mult,
                ALU.subtract, h)
            q = act(mem_sq[m % 4][:, :], memT[:, m, :], ACT.Square)
            tt(G, mem_sum[:, :], mem_sum[:, :], mem_sq[m % 4][:, :], ALU.add, q, G.now())

    def gate_tile(g):
        return GATE0 + g if g < 3 * FT else g - 3 * FT

    def leave_merge(ga, gb, op):
        def make(m, before):
            def leave(ps, freed, out_, j):
                V.need(*before)
                g1 = V.did(V.q.tensor_tensor(tmp[j][:, :], ps[0], tile(P, m + ga), ALU.mult))
                freed(V.q.tensor_tensor(sq[j][:, :], ps[1], tile(P, m + gb), ALU.mult))
                out_(G)
                g3 = tt(G, tmp[j][:, :], tmp[j][:, :], sq[j][:, :], ALU.add, g1)
                return two_parts(op, m, tmp[j][:, :], g3)
            return leave
        return make

    fill(G, mem_sum[:, :], 0.0, V.now())
    merged = []
    for b0, n in ((0, 4), (4, 4)):
        def make(m, before, b0=b0):
            return leave_merge(GATE0, gate_tile(8 + b0) - b0, opB)(m + b0, before)
        merged += segment(n, opA, make, two=True, ready=[None] * KT if b0 else ready,
                          between=lambda b0=b0: memory_parts(range(b0, b0 + 4)), act=1, dve=2, pool=1)

    V.need(m_x)
    A.need(m_x)
    attn_in = segment(KT, opB, leave_residual("norm_xattn", opA), ready=merged,
                      between=lambda: rms(n=N_MEM, dst=rstd_m, sums=(mem_sum,), clear=False), act=2, dve=1, pool=1)

    segment(2 * KT, memo, leave_plain(kvT, rstd_m[:, :]), n=N_MEM)
    segment(KT, opA, leave_plain(qT, rstd[:, :]), ready=attn_in, between=rms)
    for E in (T, A, V):
        E.q.wait_ge(s_free, panel_no.n + 2)
    for mt in range(2):
        b = 2 + mt
        for g in range(2):
            for q in range(4):
                ins = nc.tensor.transpose(bank[b + 2 * g][:, q * NP:(q + 1) * NP],
                                          kvT[:, KT + 4 * g + q, mt * NP:(mt + 1) * NP], mat("ident"))
            m = T.did(ins)
            copy(A, vtm[:, mt, g * 512:(g + 1) * 512], bank[b + 2 * g][:, :], m)

    ex = [place(f"exp{n}", [NP, 4, N_MEM], r_p + (32 + 2 * n) * TB) for n in range(2)]
    pT = [place(f"probs_t{n}", [NP, 2, S], r_p + (4 if n else 36) * TB) for n in range(2)]
    stat = [place(f"stat{n}", [NP, 16], r_pb + n * 64) for n in range(2)]
    XS = XD ** -0.5
    score_free, tr_free, pv_free = {}, {}, {}
    sm, prob = {}, {}

    def scores(h):
        n, e = h % 2, ex[h % 2]
        mx, nm, su, rs = (stat[n][:, 4 * q:4 * q + 4] for q in range(4))
        ms = []
        for half in range(2):
            b = 2 * n + half
            T.need(score_free.get(b))
            for q in range(2):
                t = 2 * half + q
                for d in range(2):
                    ins = mm(bank[b][:, q * N_MEM:(q + 1) * N_MEM], qT[:, 2 * h + d, t * NP:(t + 1) * NP],
                             kvT[:, 2 * h + d, :], start=(d == 0), stop=(d == 1))
            m = T.did(ins)
            V.need(m, *([sm[h - 2]] if h >= 2 else []))
            ms.append(V.did(V.q.reduce_max(mx[:, 2 * half:2 * half + 2],
                                           bank[b][:, :].rearrange("p (t m) -> p t m", t=2), AX.X)))
        nmm = ts(V, nm, mx, -XS, ALU.mult, None, None, *ms)
        for t in range(4):
            b = 2 * n + t // 2
            A.need(nmm, prob.get(h - 2))
            score_free[b] = A.did(A.q.activation(e[:, t, :], bank[b][:, (t % 2) * N_MEM:(t % 2 + 1) * N_MEM], ACT.Exp,
                                                 bias=nm[:, t:t + 1], scale=XS, accum_out=su[:, t:t + 1]))
        V.need(score_free[2 * n + 1])
        r = V.did(V.q.reciprocal(rs, su))
        sm[h] = tt(V, e[:, :, :], e[:, :, :], rs.unsqueeze(2).broadcast_to([NP, 4, N_MEM]), ALU.mult, r)

    pts = {}

    def turn(h):
        n = h % 2
        T.need(sm[h])
        pts[h] = []
        for mt in range(2):
            b = 4 + mt
            T.need(tr_free.get(b))
            for t in range(4):
                ins = nc.tensor.transpose(bank[b][:, t * NP:(t + 1) * NP], ex[n][:, t, mt * NP:(mt + 1) * NP], mat("ident"))
            m = T.did(ins)
            prob[h] = m
            tr_free[b] = copy(A if mt else V, pT[n][:, mt, :], bank[b][:, :], m, pv_free.get((h - 2, 1)))
            pts[h].append(tr_free[b])

    def weigh(h):
        n = h % 2
        for d in range(2):
            b = 6 + d
            T.need(*pts[h], pv_free.get((h - 1, d, "out")))
            for mt in range(2):
                c = h * XD + d * NP
                ins = mm(bank[b][:, :], vtm[:, mt, c:c + NP], pT[n][:, mt, :], start=(mt == 0), stop=(mt == 1))
            m = T.did(ins)
            pv_free[(h, 1)] = m
            hi = act(opB[0][:, 2 * h + d, :], bank[b][:, :], ACT.Copy, m)
            pv_free[(h, d, "out")] = tt(V, opB[1][:, 2 * h + d, :], bank[b][:, :],
                                        opB[0][:, 2 * h + d, :].bitcast(F32), ALU.subtract, hi)

    T.need(A.now())
    scores(0)
    scores(1)
    for h in range(XH):
        turn(h)
        if h + 2 < XH:
            scores(h + 2)
        weigh(h)
    for E in (T, A, V):
        E.need(A.now(), V.now())

    mlp_in = segment(KT, opB, leave_residual("norm_mlp", opA), act=2, dve=1, pool=1)

    AW = 3 * D
    ada_sum = place("ada_sum", [NP, AW], r_p)
    ada_in = [place(f"ada_w{n}", [NP, AW], r_p + (6 + 6 * n) * TB) for n in range(2)]
    s_ada = [nc.alloc_semaphore(f"ada_rows{n}") for n in range(2)]
    c0 = act(silc, vecs[:, COL["c"]:COL["c"] + 8], ACT.Sigmoid)
    c1 = tt(V, silc, silc, vecs[:, COL["c"]:COL["c"] + 8], ALU.mult, c0)
    at_start = [c1, A.now(), V.now(), T.now()]

    def modulation():
        G.need(*at_start)
        for k in range(KT):
            n = k % 2
            if k >= 2:
                G.need(G.now())
            if k == 0:
                for q in range(2):
                    nc.gpsimd.dma_start(ada_in[q][:, :], ada_w[q * NP:(q + 1) * NP, :]).then_inc(s_ada[q], 16)
            nc.gpsimd.wait_ge(s_ada[n], 16 * (k // 2 + 1))
            if k == 0:
                ts(G, ada_sum[:, :], ada_in[0][:, :], silc[:, 0:1], ALU.mult, None, None)
            else:
                a1 = ts(G, ada_in[n][:, :], ada_in[n][:, :], silc[:, k:k + 1], ALU.mult, None, None, G.now())
                tt(G, ada_sum[:, :], ada_sum[:, :], ada_in[n][:, :], ALU.add, a1, G.now())
            if k + 2 < KT:
                G.need(G.now())
                nc.gpsimd.dma_start(ada_in[n][:, :], ada_w[(k + 2) * NP:(k + 3) * NP, :]).then_inc(s_ada[n], 16)

    hid = [place(f"hidden{j}", [NP, S], r_p + (24 + j) * TB) for j in range(2)]

    def leave_relu2(m, before):
        def leave(ps, freed, out_, j):
            V.need(*before)
            freed(V.q.scalar_tensor_tensor(tmp[j][:, :], ps[0], 0.0, rstd[:, :], ALU.max, ALU.mult))
            out_(A)
            out_(V)
            h = A.did(A.q.activation(opB[0][:, bass.ds(m, 1), :].rearrange("p a n -> p (a n)"), tmp[j][:, :], ACT.Square))
            h2 = tt(V, hid[j][:, :], tmp[j][:, :], tmp[j][:, :], ALU.mult)
            return tt(V, tile(opB[1], m), hid[j][:, :], tile(opB[0], m).bitcast(F32), ALU.subtract, h, h2)
        return leave

    def leave_relu2_make(m, before):
        return leave_relu2(m, [before[0], before[1]])

    segment(KT, opA, leave_relu2_make, act=1, dve=2, ready=mlp_in,
            between=lambda: (rms(), modulation()))
    hid_done = [2 * (KT - 1 - k) for k in range(KT)]
    with loop(nc, lanes, 3, panels=16, act=8, dve=16):
        segment(KT, opB, leave_residual(), ready=[V.ago(d) for d in hid_done])
        segment(KT, opA, leave_relu2_make, act=1, dve=2)

    hid_done = [V.ago(d) for d in hid_done]
    T.need(G.now())
    for c in range(24):
        ins = mm(bank[6][:, c:c + 1], ada_sum[:, c * NP:(c + 1) * NP], mat("mean")[:, 0:1])
    m = T.did(ins)
    d0 = stt(adac, bank[6][:, 0:24], float(D), vecs[:, COL["b_ada"]:COL["b_ada"] + 24], ALU.mult, ALU.add, m)
    d1 = stt(gain2, adac[:, 8:16], 1.0, vecs[:, COL["g_pre"]:COL["g_pre"] + 8], ALU.add, ALU.mult, d0)
    d3 = tt(V, gain3, gain2, vecs[:, COL["norm_final"]:COL["norm_final"] + 8], ALU.mult, d1)
    d2 = tt(V, gate2, adac[:, 16:24], vecs[:, COL["g_post"]:COL["g_post"] + 8], ALU.mult, d0)

    fill(G, acc2[:, :], 0.0, A.now(), V.now())

    def leave_x3(m, before):
        def leave(ps, freed, out_, j):
            freed(V.q.tensor_tensor(tile(xT, m), ps[0], tile(xT, m), ALU.add))
            out_(A)
            s1 = act(sq[j][:, :], tile(xT, m), ACT.Square, *before)
            s2 = act(tmp[j][:, :], tile(xT, m), ACT.Square, scale=vec("norm_final", m))
            tt(G, acc[:, :], acc[:, :], sq[j][:, :], ALU.add, s1, G.now())
            tt(G, acc2[:, :], acc2[:, :], tmp[j][:, :], ALU.add, s2, G.now())
        return leave
    segment(KT, opB, leave_x3, ready=hid_done, act=2, pool=2)

    T.need(G.now(), V.now())
    token_cols(acc, bank[7])
    m1 = token_cols(acc2, bank[6])
    rc, r1c = head_cols[:, 0:4], head_cols[:, 4:8]
    e1 = ts(V, r1c, bank[7][:, 0:4], EPS, ALU.add, None, None, m1)
    e2 = stt(rc, r1c, EPS, bank[6][:, 0:4], ALU.mult, ALU.add, e1)
    e3 = act(head_cols, head_cols, ACT.Sqrt, e2)
    V.need(e3)
    e4 = V.did(V.q.reciprocal(head_cols, head_cols))
    r = token_wide(rc, rstd, bank[5], e4)
    ready, h0, h1 = [], {}, {}

    def scaled_tile(k):
        h0[k] = stt(tmp[k % 2][:, :], xT[:, k, :], gain3[:, k:k + 1], bank[5][:, :], ALU.mult, ALU.mult, r,
                    h1.get(k - 2), V.now())
    for k in range(2):
        scaled_tile(k)
    for k in range(KT):
        h1[k] = act(opA[0][:, k, :], tmp[k % 2][:, :], ACT.Identity, h0[k], bias=adac[:, k:k + 1])
        ready.append(stt(opA[1][:, k, :], tmp[k % 2][:, :], adac[:, k:k + 1], opA[0][:, k, :].bitcast(F32), ALU.add,
                         ALU.subtract, h1[k]))
        if k + 2 < KT:
            scaled_tile(k + 2)

    def x4():
        m = token_wide(r1c, r1, bank[6])
        for k in range(KT):
            stt(xT[:, k, :], xT[:, k, :], vec("norm_final", k), bank[6][:, :], ALU.mult, ALU.mult, m)
    segment(7, opA, leave_copy(0), ready=ready, between=x4)
    qkv_out = panel_no.n + 2

    scores_at, probs_at = r_opB + 12 * TB, r_opB + 4 * TB
    posi = place("positions_i", [NP, S], probs_at, I32)
    ang, nr = (place(f"angle{n}", [NP, S], probs_at + (1 + n) * TB) for n in range(2))
    rot = [place(f"rotated{n}", [NP, S], scores_at + n * TB) for n in range(2)]
    cosT, sinT = sq
    kd = [place(f"k_dup{g}", [NP, NP + S], r_p + 35 * TB + g * (NP + S) * 4) for g in range(2)]
    vb2 = place("v2_t", [NP, 4, NP], r_acc)
    wm = place("window_masks", [NP, 512], r_pad)
    sinkb = place("sinks", [NP, 8], r_st)
    A.need(T.now(), V.now(), G.now())
    m_pos = load("positions", (posi[:, :], pos_in))
    m_sink = load("sinks_and_masks", (sinkb[:, :], sink_in), (wm[:, :], win_in))
    TURN, MAGIC = 2 * np.pi, 1.5 * 2 ** 23
    T1 = 6.28125
    T2 = 0.0019350051879882812
    T3 = TURN - T1 - T2

    def angle(dst, quarter):
        n0 = ts(V, nr[:, :], ang[:, :], 1 / TURN, ALU.mult, quarter, ALU.add, V.now())
        n1 = ts(V, nr[:, :], nr[:, :], MAGIC, ALU.add, None, None, n0)
        n2 = ts(V, nr[:, :], nr[:, :], -MAGIC, ALU.add, None, None, n1)
        n3 = stt(dst[:, :], nr[:, :], -T1, ang[:, :], ALU.mult, ALU.add, n2)
        n4 = stt(dst[:, :], nr[:, :], -T2, dst[:, :], ALU.mult, ALU.add, n3)
        n5 = stt(dst[:, :], nr[:, :], -T3, dst[:, :], ALU.mult, ALU.add, n4)
        n6 = ts(V, dst[:, :], dst[:, :], quarter * TURN, ALU.add, 3.1415925, ALU.min, n5)
        n7 = ts(V, dst[:, :], dst[:, :], -3.1415925, ALU.max, None, None, n6)
        act(dst[:, :], dst[:, :], ACT.Sin, n7)

    def sines():
        r0 = copy(V, ang[:, :], posi[:, :], m_pos, G.now(), A.now())
        ts(V, ang[:, :], ang[:, :], vec("inv_freq"), ALU.mult, None, None, r0)
        angle(sinT, 0.0)

    def cosines():
        angle(cosT, 0.25)
        for g in range(2):
            fill(G, kd[g][:, 0:NP], 0.0)

    done_b = {}

    def rope(n, dst, t):
        b = 6 + n % 2
        T.need(done_b.get(b))
        m = T.did(mm(bank[b][:, :], mat("rotate"), P[:, t, :]))
        e = tt(G, dst, P[:, t, :], cosT[:, :], ALU.mult, trig, m)
        d = tt(V, rot[n % 2][:, :], bank[b][:, :], sinT[:, :], ALU.mult, m, trig, V.now())
        done_b[b] = d
        tt(V, dst, dst, rot[n % 2][:, :], ALU.add, e, d)

    def rope_keys():
        for E in (T, G):
            E.q.wait_ge(s_free, qkv_out)
        for g in range(2):
            rope(g, kd[g][:, NP:], KD2 + g)
        rope(2, P[:, 0, :], 0)

    def rope_queries():
        for t in range(1, 4):
            rope(2 + t, P[:, t, :], t)
        T.need(done_b[6])
        for n in range(4):
            ins = nc.tensor.transpose(bank[6][:, n * NP:(n + 1) * NP], P[:, V2, n * NP:(n + 1) * NP], mat("ident"))
        m = T.did(ins)
        copy(A, vb2[:, :, :], bank[6][:, :].rearrange("p (n d) -> p n d", n=4), m)

    segment(4, opA, leave_function(UB, ACT.Gelu), between=sines)
    segment(4, opA, leave_function(VB, ACT.Gelu), between=cosines)
    trig = A.now()
    segment(4, opA, leave_silu(ZA), between=rope_keys, act=1)
    segment(4, opA, leave_silu(ZB), between=rope_queries, act=1)

    gate_pieces = []

    def gate_leave(e, before):
        def leave(ps, freed, out_, j):
            A.need(*before)
            freed(A.q.activation(P[:, G2 + e, :], ps[0], ACT.Sigmoid))
        return leave

    def filler2(count):
        for _ in range(count):
            e, k = divmod(len(gate_pieces), KT)
            if e < N_IN2 - G2:
                steps = (gate_pieces[-1] if k else
                         panel_steps(opA, gate_leave(e, [T.now(), V.now(), G.now()] if G2 + e >= 35 else [])))
                next(steps)
                gate_pieces.append(steps)

    sc = place("scores2", [NP, 8, 257], scores_at)
    pt2 = place("probs2_t", [NP, 16, NP], probs_at)
    stat2 = place("stat2", [NP, 32], r_pb)
    mx, nm, su, rs = (stat2[:, 8 * q:8 * q + 8] for q in range(4))
    maskv = wm[:, :].rearrange("p (a j) -> p a j", a=2)
    zb_out = panel_no.n + 2
    filler2(2)
    T.need(A.now(), V.now(), G.now())
    for E in (A, V, G):
        E.q.wait_ge(s_free, zb_out)
        E.need(A.now(), V.now(), G.now(), m_sink)
    tr_done = out_done = None
    for t in range(4):
        g = t // 2
        G.need(tr_done, A.now())
        sk = copy(G, sc[:, :, 256:257].rearrange("p (n h) a -> p n (h a)", h=2),
                  sinkb[:, 2 * t:2 * t + 2].unsqueeze(1).broadcast_to([NP, 4, 2]))
        ss = []
        for i2 in range(2):
            for q in range(2):
                n = 2 * i2 + q
                for h, (lo, hi) in enumerate(HH):
                    ins = mm(bank[2 + 2 * i2 + h][:, q * 256:(q + 1) * 256], P[lo:hi, t, n * NP:(n + 1) * NP],
                             kd[g][lo:hi, n * NP:n * NP + 256])
            m = T.did(ins)
            mk = maskv if i2 == 0 else maskv[:, 1, :].unsqueeze(1).broadcast_to([NP, 2, 256])
            for h in range(2):
                ss.append(stt(sc[:, 4 * i2 + h:4 * i2 + h + 3:2, 0:256],
                              bank[2 + 2 * i2 + h][:, :].rearrange("p (q j) -> p q j", q=2),
                              HD ** -0.5, mk, ALU.mult, ALU.add, m, tr_done))
        V.need(*ss, sk, A.now())
        x0 = V.did(V.q.reduce_max(mx, sc[:, :, :], AX.X))
        x1_ = ts(V, nm, mx, -1.0, ALU.mult, None, None, x0)
        filler2(F2_MAX)
        for e in range(8):
            A.need(x1_)
            ea = A.did(A.q.activation(sc[:, e, :], sc[:, e, :], ACT.Exp, bias=nm[:, e:e + 1], accum_out=su[:, e:e + 1]))
        V.need(ea)
        x2_ = V.did(V.q.reciprocal(rs, su))
        x3_ = tt(V, sc[:, :, 0:256], sc[:, :, 0:256], rs.unsqueeze(2).broadcast_to([NP, 8, 256]), ALU.mult, x2_)
        filler2(F2_SOFTMAX)
        T.need(x3_)
        pts = []
        for n in range(4):
            for h in range(2):
                for jt in range(2):
                    ins = nc.tensor.transpose(bank[2 + n][:, (2 * h + jt) * NP:(2 * h + jt + 1) * NP],
                                              sc[:, 2 * n + h, jt * NP:(jt + 1) * NP], mat("ident"))
            m = T.did(ins)
            pts.append(copy(A if n % 2 else V, pt2[:, 4 * n:4 * n + 4, :],
                            bank[2 + n][:, :].rearrange("p (a q) -> p a q", a=4), m, out_done))
        tr_done = T.now()
        filler2(F2_OUT)
        b = 6 + t % 2
        T.need(*pts)
        first = [True, True]
        for n in range(4):
            for h, (lo, hi) in enumerate(HH):
                for jt in range(2):
                    if n == 0 and jt == 0:
                        continue
                    ins = mm(bank[b][lo:hi, n * NP:(n + 1) * NP], vb2[:, n - 1 + jt, g * HD:(g + 1) * HD],
                             pt2[:, 4 * n + 2 * h + jt, :], start=first[h], stop=(n == 3 and jt == 1))
                    first[h] = False
        m = T.did(ins)
        out_done = m
        ya = tt(V, P[:, ZA + t, :], bank[b][:, :], P[:, ZA + t, :], ALU.mult, m)
        two_parts(opB, t, P[:, ZA + t, :], ya)

    vn = place("v_norm", [NP, 4, HALF], r_p)
    lng, lnb = (place(n, [NP, HALF], r_p + (4 + j) * TB) for j, n in enumerate(("ln_v_g", "ln_v_b")))
    bsb = place("b_s", [NP, 4, NP], r_p + 6 * TB)
    wsr, wst = (place(n, [NP, 4, NP], r_sq + j * TB) for j, n in enumerate(("w_s", "w_s_t")))
    for E in (A, V, G):
        E.need(A.now(), V.now(), G.now(), T.now())
    m_sg = load("spatial_gating", (lng[:, :], lnv_in[0]), (lnb[:, :], lnv_in[1]),
                (bsb[:, :, :].rearrange("p g t -> p (g t)"), bs_in), (wsr[:, :, :], ws_in.rearrange("g t s -> t g s")))
    V.need(m_sg)
    G.need(m_sg)
    st6 = place("bn6", [NP, 4, 6], r_st + 64)
    mv = place("bn_mv", [NP, 4, 2], r_st + 256)
    vnd, cp = [], []
    T.need(V.now(), A.now())
    for n in range(4):
        for q in range(4):
            ins = nc.tensor.transpose(bank[2 + n][:, q * NP:(q + 1) * NP], P[:, VB + q, n * NP:(n + 1) * NP], mat("ident"))
        cp.append(T.did(ins))
    for n in range(4):
        c0 = copy(A, vn[:, n, :], bank[2 + n][:, :], cp[n])
        V.need(c0)
        c1 = V.did(V.q.bn_stats(st6[:, n, :], vn[:, n, :]))
        V.need(c1)
        vnd.append(V.did(V.q.bn_aggr(mv[:, n, :], st6[:, n, :])))
    c3 = inv_sqrt(mv[:, :, 1:2], mv[:, :, 1:2], 1.0, ALU.add, EPS, *vnd)
    vnd = []
    for n in range(4):
        c4 = ts(V, vn[:, n, :], vn[:, n, :], mv[:, n, 0:1], ALU.subtract, mv[:, n, 1:2], ALU.mult, c3)
        E = (V, G)[n % 2]
        c5 = tt(E, vn[:, n, :], vn[:, n, :], lng[:, :], ALU.mult, c4)
        vnd.append(tt(E, vn[:, n, :], vn[:, n, :], lnb[:, :], ALU.add, c5))
    T.need(m_sg)
    for g in range(4):
        ins = nc.tensor.transpose(bank[6][:, g * NP:(g + 1) * NP], wsr[:, g, :], mat("ident"))
    m = T.did(ins)
    wsd = tt(V, wst[:, :, :], bank[6][:, :].rearrange("p (g t) -> p g t", g=4), wide("causal", 4), ALU.mult, m)
    uz = [tt(G, P[:, UB + g, :], P[:, UB + g, :], P[:, ZB + g, :], ALU.mult) for g in range(4)]
    filler2(KT * (N_IN2 - G2) - F2_LAST - len(gate_pieces))
    T.need(*vnd, wsd)
    sv = []
    for g in range(4):
        for n in range(4):
            ins = mm(bank[2 + g][:, n * NP:(n + 1) * NP], vn[:, n, g * NP:(g + 1) * NP], wst[:, g, :])
        sv.append(T.did(ins))
    ready = [V.now()] * 4
    for g in range(4):
        j = g % 2
        e0 = tt(V, tmp[j][:, :].rearrange("p (n t) -> p n t", n=4), bank[2 + g][:, :].rearrange("p (n t) -> p n t", n=4),
                bsb[:, g, :].unsqueeze(1).broadcast_to([NP, 4, NP]), ALU.add, sv[g], V.now(), A.now())
        e1 = tt(V, tmp[j][:, :], tmp[j][:, :], P[:, UB + g, :], ALU.mult, e0, uz[g])
        ready.append(two_parts(opB, 4 + g, tmp[j][:, :], e1))
    filler2(F2_LAST)

    fill(G, acc[:, :], 0.0, T.now())
    V.q.wait_ge(s_free, panel_no.n + 2)
    merged = segment(KT, opB, leave_merge(G2, G2 + 8, opA), two=True, ready=ready, act=1, dve=2, pool=1)

    def leave_final(m, before):
        def leave(ps, freed, out_, j):
            s = act(sq[j][:, :], ps[0], ACT.Square, *before)
            V.need(s)
            freed(V.q.tensor_scalar(tile(P, m), ps[0], gate2v(m), None, ALU.mult))
            tt(G, acc[:, :], acc[:, :], sq[j][:, :], ALU.add, s, G.now())
        return leave

    def gate2v(m):
        return gate2[:, m:m + 1] if isinstance(m, int) else gate2[:, bass.ds(m, 1)]
    segment(KT, opA, leave_final, ready=merged, last=1, act=1, pool=1)
    T.need(G.now())
    m = ts(V, head_cols[:, 0:4], bank[7][:, 0:4], EPS, ALU.add, None, None, token_cols(acc, bank[7]))
    V.need(act(head_cols[:, 0:4], head_cols[:, 0:4], ACT.Sqrt, m))
    m = V.did(V.q.reciprocal(head_cols[:, 0:4], head_cols[:, 0:4]))
    V.q.wait_ge(s_free, panel_no.n + 2)
    rdone = token_wide(head_cols[:, 0:4], rstd, bank[6], m)
    s_out = nc.alloc_semaphore("stored")
    for k in range(KT):
        z0 = tt(V, P[:, k, :], P[:, k, :], bank[6][:, :], ALU.mult, rdone)
        z1 = tt(G if k in (0, 2, 4) else V, xT[:, k, :], xT[:, k, :], P[:, k, :], ALU.add, z0)
        nc.sync.wait_ge(z1.sem, z1.value())
        nc.sync.dma_start(out[k * NP:(k + 1) * NP, :], xT[:, k, :]).then_inc(s_out, 16)
    nc.sync.wait_ge(s_out, 16 * KT)
    for E in (T, G):
        nc.sync.wait_ge(E.passed.sem, E.passed.n)
    assert panel_no.n == n_panels, (panel_no.n, n_panels)


F2_MAX, F2_SOFTMAX, F2_OUT, F2_LAST = 8, 10, 3, 14
F_START, F_NORM, F_X, F_SOLVE, F_CHAIN, F_TAIL, F_TAIL2, F_AB = 2, 4, 2, 1, 1, 3, 5, 3
WKV_PE, WKV_ACT, WKV_DVE, WKV_POOL = 61, 31, 70, 7


def tiles_of(v):
    return np.asarray(v).reshape(-1, NP).T


def panelled(w):
    k, n = w.shape
    return w.reshape(k // NP, NP, n // NP, NP).transpose(2, 1, 0, 3).reshape(n // NP, NP, k)


def layout(i):
    w_in = i["w_in"][0]
    rw = np.concatenate([w_in[:, 0:1824], np.zeros((D, N_RW * NP - 1824), w_in.dtype)], axis=1)
    rw = panelled(rw)
    rest = panelled(w_in[:, 1824:])
    conv, gates = rest[0:12], rest[12:28]
    mixed = []
    for f in range(FT):
        mixed += [conv[f], conv[4 + f], conv[8 + f], *gates[3 * f:3 * f + 3]]
    mixed += list(gates[12:16])
    proj = panelled(np.concatenate([i["w_proj_a"][0], i["w_proj_b"][0]], axis=0))
    mlp = []
    for c in range(4):
        mlp += [panelled(i["w_up"][0][:, c * D:(c + 1) * D]), panelled(i["w_down"][0][c * D:(c + 1) * D, :])]
    w2 = i["w_in_2"][0]
    o = np.cumsum([0, 512, 128, 128, 512, 512, 512, 512, 2048])
    q, k, v, za, ub, vb, zb, gl = (w2[:, a:b] for a, b in zip(o[:-1], o[1:]))
    k0, k1 = k[:, 0:64], k[:, 64:128]
    in2 = panelled(np.concatenate([q, k0, k0, k1, k1, v, ub, vb, za, zb, gl], axis=1))
    proj2 = panelled(np.concatenate([i["w_proj_a_2"][0], i["w_proj_b_2"][0]], axis=0))
    panels = np.concatenate([rw, np.stack(mixed), proj, panelled(i["w_out_mix"][0]), panelled(i["w_kv"][0]),
                             panelled(i["w_q"][0]), panelled(i["w_xo"][0]), *mlp, in2, proj2,
                             panelled(i["w_out_2"][0])])
    mu = np.concatenate([i["mu_shift"][0], np.zeros(N_RW * NP - 1824, np.float32)])
    half = HD // 2
    freq = (np.float32(10000.0) ** (-np.arange(half, dtype=np.float32) / np.float32(half))).astype(np.float32)
    parts = {
        "norm_mix": i["norm_mix"][0], "b_gate": i["b_gate"][0], "mu": mu, "a0": i["a0"][0],
        "k_k": i["k_k"][0], "k_a": i["k_a"][0], "r_k": i["r_k"][0].reshape(-1), "ln_x_w": i["ln_x_w"][0],
        "ln_x_b": i["ln_x_b"][0], "conv_w": i["conv_w"][0].reshape(-1), "norm_xattn": i["norm_xattn"][0],
        "norm_mem": i["norm_mem"][0], "norm_mlp": i["norm_mlp"][0], "norm_final": i["norm_final"],
        "g_pre": i["g_pre_2"][0], "g_post": i["g_post_2"][0], "b_ada": i["b_ada_2"][0], "c": i["c_2"][0],
        "inv_freq": np.tile(freq, 4),
    }
    vec = np.concatenate([tiles_of(parts[n]) for n, _ in VECS], axis=1)
    lora = np.concatenate([i["w_lora_w"][0], i["w0"][0][None], i["w_lora_a"][0], i["w_lora_g"][0]], axis=0)
    wide = lambda v: np.broadcast_to(np.asarray(v).reshape(1, -1), (NP, np.asarray(v).size))
    arrays = {
        "x": i["x"][0].T, "mem": i["mem"][0].T, "panels": panels, "ada": i["w_ada_2"][0], "vec": vec,
        "mat": constants(), "win": window_masks(), "lora": lora, "pos": wide(i["positions_2"][0]),
        "sink": wide(i["sinks_2"][0]), "ws": i["w_s_2"][0],
        "lnv": np.stack([wide(i["ln_v_g_2"][0]), wide(i["ln_v_b_2"][0])]), "bs": wide(i["b_s_2"][0]),
    }
    return {k: np.ascontiguousarray(v) for k, v in arrays.items()}


def kernel(**inputs):
    import concourse.bacc as bacc
    from concourse.bass_utils import run_bass_kernel_spmd

    nc = bacc.Bacc("TRN2", target_bir_lowering=False, num_devices=1)
    arrays = layout({k: np.asarray(v) for k, v in inputs.items()})
    aps = [nc.dram_tensor(k, v.shape, mybir.dt.from_np(v.dtype), kind="ExternalInput").ap() for k, v in arrays.items()]
    out = nc.dram_tensor("out", (D, S), F32, kind="ExternalOutput").ap()
    build(nc, *aps, out)
    r = run_bass_kernel_spmd(nc, [arrays], core_ids=[0])
    got = r.results[0]["out"]
    return np.ascontiguousarray(got.T)[None]
```
